# Optimizing a Trainium2 kernel written in Bass

```python
import jax
import jax.numpy as jnp
from jax import lax
import numpy as np

D_MODEL = 1024
BATCH = 1
SEQ = 512
DEPTH = 2
DEC_BATCH = 8
DEC_SEQ = 4
PAST_LEN = 1024
PAGE_SIZE = 128

HEAD_DIM = 64
RET_HEADS = 4
SWA_HEADS = 4
CONV_CH = 256
SGU_GROUPS = 4
SGU_GDIM = 64
RET_W = RET_HEADS * HEAD_DIM
SWA_W = SWA_HEADS * HEAD_DIM
SGU_W = SGU_GROUPS * SGU_GDIM
MIX_W = RET_W + SWA_W + CONV_CH + SGU_W
SPLIT_SIZES = (RET_W, RET_W, RET_W, RET_W, SWA_W, SWA_W, SWA_W, 2 * CONV_CH, 2 * SGU_W)
IN_W = 4 * RET_W + 3 * SWA_W + 2 * CONV_CH + 2 * SGU_W
RET_CHUNK = 128
RET_THETA = 10000.0
ROPE_THETA = 500000.0
ROPE_DIM = HEAD_DIM // 4
DILATED_CONFIGS = ((128, 1), (512, 4), (2048, 16))
SWA_WINDOW = 2048
DIL_BLOCK = 128
CONV_WIDTH = 31
SGU_CHUNK = 128
N_GROUPS = 4
EXPERTS_PER_GROUP = 8
N_EXPERTS = N_GROUPS * EXPERTS_PER_GROUP
TOP_K = 2
D_EXPERT = 512
MOE_BLOCK = 128
DN_ALPHA = (2 * DEPTH) ** 0.25
DN_BETA = (8 * DEPTH) ** -0.25
LN_EPS = 1e-5
NEG_INF = -1e30
F32 = jnp.float32

kernel_name = 'hybrid_retention_dilated_conv_sgu_hmoe_step'

def layer_norm(x, g, b=None):
    xf = x.astype(F32)
    mu = xf.mean(-1, keepdims=True)
    var = jnp.square(xf - mu).mean(-1, keepdims=True)
    y = (xf - mu) * lax.rsqrt(var + LN_EPS) * g.astype(F32)
    return y if b is None else y + b.astype(F32)

def rotary(x, pos, rot_dim, theta):
    half = rot_dim // 2
    inv = jnp.float32(theta) ** (-jnp.arange(half, dtype=F32) * (2.0 / rot_dim))
    ang = pos.astype(F32)[:, None] * inv[None, :]
    c = jnp.cos(ang)[None, :, None, :]
    s = jnp.sin(ang)[None, :, None, :]
    xf = x.astype(F32)
    x1, x2 = xf[..., :half], xf[..., half:rot_dim]
    return jnp.concatenate([x1 * c - x2 * s, x2 * c + x1 * s, xf[..., rot_dim:]], axis=-1)

def retention(q, k, v, s0):
    B, T, H, Dk = q.shape
    L = RET_CHUNK if T % RET_CHUNK == 0 else T
    nc = T // L
    log_g = jnp.log1p(-jnp.exp2(-5.0 - jnp.arange(H, dtype=F32)))
    i = jnp.arange(L, dtype=F32)
    rel = i[:, None] - i[None, :]
    decay = jnp.where(rel >= 0, jnp.exp(log_g[:, None, None] * jnp.maximum(rel, 0.0)), 0.0)
    q_dec = jnp.exp(log_g[:, None] * (i + 1.0))[None, :, :, None]
    k_dec = jnp.exp(log_g[:, None] * (L - 1.0 - i))[None, :, :, None]
    c_dec = jnp.exp(log_g * L)[None, :, None, None]

    def chunks(x):
        return x.astype(F32).reshape(B, nc, L, H, x.shape[-1]).transpose(1, 0, 3, 2, 4)

    def step(S, qkv):
        qc, kc, vc = qkv
        a = jnp.einsum('bhid,bhjd->bhij', qc, kc) * decay
        o = jnp.einsum('bhij,bhjd->bhid', a, vc) + jnp.einsum('bhid,bhde->bhie', qc, S) * q_dec
        S = S * c_dec + jnp.einsum('bhjd,bhje->bhde', kc * k_dec, vc)
        return S, o

    S, o = lax.scan(step, s0.astype(F32), (chunks(q), chunks(k), chunks(v)))
    o = o.transpose(1, 0, 3, 2, 4).reshape(B, T, H, -1)
    return o, S

def _band_attend(q, k, v, dil, span):
    B, T, H, Dh = q.shape
    L = T // dil
    nb = -(-L // DIL_BLOCK)
    Lp = nb * DIL_BLOCK

    def sub(x):
        x = x.reshape(B, L, dil, H, Dh)
        x = jnp.pad(x, ((0, 0), (0, Lp - L), (0, 0), (0, 0), (0, 0)))
        return x.reshape(B, nb, DIL_BLOCK, dil, H, Dh)

    def band(x):
        prev = jnp.pad(x, ((0, 0), (1, 0), (0, 0), (0, 0), (0, 0), (0, 0)))[:, :-1]
        return jnp.concatenate([prev, x], axis=2)

    qs = sub(q)
    kb = band(sub(k))
    vb = band(sub(v))
    s = jnp.einsum('bnqrhd,bnkrhd->bnrhqk', qs, kb) * (HEAD_DIM ** -0.5)
    qi = jnp.arange(DIL_BLOCK)
    ki = jnp.arange(2 * DIL_BLOCK)
    blk = jnp.arange(nb)
    rel = DIL_BLOCK + qi[:, None] - ki[None, :]
    valid = (rel >= 0) & (rel <= span)
    valid = valid[None] & ((blk[:, None, None] * DIL_BLOCK - DIL_BLOCK + ki[None, None, :]) >= 0)
    s = jnp.where(valid[None, :, None, None], s, NEG_INF)
    m = s.max(-1, keepdims=True)
    p = jnp.exp(s - m)
    l = p.sum(-1)
    o = jnp.einsum('bnrhqk,bnkrhd->bnqrhd', p, vb) / jnp.transpose(l, (0, 1, 4, 2, 3))[..., None]
    lse = jnp.transpose(m[..., 0] + jnp.log(l), (0, 1, 4, 2, 3))
    o = o.reshape(B, Lp, dil, H, Dh)[:, :L].reshape(B, T, H, Dh)
    lse = lse.reshape(B, Lp, dil, H)[:, :L].reshape(B, T, H)
    return o, lse

def _gather_attend(q, kc, vc, past, dil, span):
    Tn = q.shape[1]
    idx = past + jnp.arange(Tn)[:, None] - dil * jnp.arange(span + 1)[None, :]
    valid = idx >= 0
    idx = jnp.maximum(idx, 0)
    kg = kc[:, idx]
    vg = vc[:, idx]
    s = jnp.einsum('bthd,btjhd->bthj', q, kg) * (HEAD_DIM ** -0.5)
    s = jnp.where(valid[None, :, None, :], s, NEG_INF)
    m = s.max(-1, keepdims=True)
    p = jnp.exp(s - m)
    l = p.sum(-1)
    o = jnp.einsum('bthj,btjhd->bthd', p, vg) / l[..., None]
    return o, m[..., 0] + jnp.log(l)

def dilated_attention(q, k, v, k_buf, v_buf):
    outs, lses = [], []
    if k_buf is not None:
        past = k_buf.shape[1]
        kc = jnp.concatenate([k_buf.astype(F32), k], axis=1)
        vc = jnp.concatenate([v_buf.astype(F32), v], axis=1)
    for window, dil in DILATED_CONFIGS:
        span = window // dil
        if k_buf is None:
            o, lse = _band_attend(q, k, v, dil, span)
        else:
            o, lse = _gather_attend(q, kc, vc, past, dil, span)
        outs.append(o)
        lses.append(lse)
    w = jax.nn.softmax(jnp.stack(lses), axis=0)
    return jnp.einsum('cbth,cbthd->bthd', w, jnp.stack(outs))

def conv_module(a, buf, conv_w, conv_b, ln_g, ln_b):
    a = a.astype(F32)
    val, gate = jnp.split(a, 2, axis=-1)
    glu = val * jax.nn.sigmoid(gate)
    if buf is None:
        ctx = jnp.pad(glu, ((0, 0), (CONV_WIDTH - 1, 0), (0, 0)))
    else:
        ctx = jnp.concatenate([buf.astype(F32), glu], axis=1)
    y = lax.conv_general_dilated(ctx, conv_w.astype(F32)[:, None, :], (1,), 'VALID',
                                 dimension_numbers=('NWC', 'WIO', 'NWC'),
                                 feature_group_count=CONV_CH) + conv_b.astype(F32)
    return jax.nn.silu(layer_norm(y, ln_g, ln_b)), glu

def spatial_gating(uv, ln_g, ln_b, ws, bs):
    B, T, _ = uv.shape
    u, v = jnp.split(jax.nn.gelu(uv.astype(F32)), 2, axis=-1)
    vn = layer_norm(v.reshape(B, T, SGU_GROUPS, SGU_GDIM),
                    ln_g.reshape(SGU_GROUPS, SGU_GDIM), ln_b.reshape(SGU_GROUPS, SGU_GDIM))
    nc = -(-T // SGU_CHUNK)
    Tp = nc * SGU_CHUNK
    vp = jnp.pad(vn, ((0, 0), (0, Tp - T), (0, 0), (0, 0))).reshape(B, nc, SGU_CHUNK, SGU_GROUPS, SGU_GDIM)
    wm = ws.astype(F32) * jnp.tril(jnp.ones((SGU_CHUNK, SGU_CHUNK), F32))
    z = jnp.einsum('gts,bnsgc->bntgc', wm, vp) + bs.astype(F32).T[None, None, :, :, None]
    z = z.reshape(B, Tp, SGU_W)[:, :T]
    return u * z, vn.reshape(B, T, SGU_W)

def hier_moe(x, rg_w, rg_b, re_w, re_b, w1, w3, w2):
    B, T, D = x.shape
    n_tok = B * T
    xt = x.reshape(n_tok, D)
    xf = xt.astype(F32)
    g_logits = xf @ rg_w.astype(F32) + rg_b.astype(F32)
    g_sel = jnp.argmax(g_logits, axis=-1)
    g_gate = jax.nn.softmax(g_logits, axis=-1).max(-1)
    e_all = jnp.einsum('td,gde->tge', xf, re_w.astype(F32)) + re_b.astype(F32)
    e_logits = e_all[jnp.arange(n_tok), g_sel]
    e_val, e_idx = lax.top_k(e_logits, TOP_K)
    gate = jax.nn.softmax(e_val, axis=-1) * g_gate[:, None]
    expert = (g_sel[:, None] * EXPERTS_PER_GROUP + e_idx).astype(jnp.int32)
    n_asg = n_tok * TOP_K
    flat_e = expert.reshape(-1)
    flat_tok = jnp.repeat(jnp.arange(n_tok, dtype=jnp.int32), TOP_K)
    order = jnp.argsort(flat_e)
    se = flat_e[order]
    counts = jnp.bincount(flat_e, length=N_EXPERTS).astype(jnp.int32)
    start = jnp.cumsum(counts) - counts
    pcounts = (counts + MOE_BLOCK - 1) // MOE_BLOCK * MOE_BLOCK
    pstart = jnp.cumsum(pcounts) - pcounts
    dest_sorted = pstart[se] + jnp.arange(n_asg, dtype=jnp.int32) - start[se]
    dest = jnp.zeros((n_asg,), jnp.int32).at[order].set(dest_sorted)
    n_blk = -(-n_asg // MOE_BLOCK) + N_EXPERTS
    slot_tok = jnp.full((n_blk * MOE_BLOCK,), n_tok, jnp.int32).at[dest].set(flat_tok)
    blk_e = jnp.clip(jnp.searchsorted(pstart, jnp.arange(n_blk, dtype=jnp.int32) * MOE_BLOCK, side='right') - 1,
                     0, N_EXPERTS - 1)
    xpad = jnp.concatenate([xt, jnp.zeros((1, D), xt.dtype)], axis=0)

    def expert_block(args):
        tok, e = args
        xb = xpad[tok]
        return (jax.nn.silu(xb @ w1[e]) * (xb @ w3[e])) @ w2[e]

    y_slots = lax.map(expert_block, (slot_tok.reshape(n_blk, MOE_BLOCK), blk_e)).reshape(-1, D)
    y = jnp.einsum('tk,tkd->td', gate, y_slots[dest].reshape(n_tok, TOP_K, D).astype(F32))
    return y.reshape(B, T, D)

def token_mixers(x, pos, w_in, w_out, ret_gn_g, conv_w, conv_b, conv_ln_g, conv_ln_b,
                 sgu_ln_g, sgu_ln_b, sgu_w, sgu_b, layer_cache):
    B, T, _ = x.shape
    h = x @ w_in
    cuts, acc = [], 0
    for size in SPLIT_SIZES[:-1]:
        acc += size
        cuts.append(acc)
    rq, rk, rv, rg, sq, sk, sv, conv_in, sgu_in = jnp.split(h, cuts, axis=-1)

    def heads(t):
        return t.reshape(B, T, -1, HEAD_DIM)

    if layer_cache is None:
        s0 = jnp.zeros((B, RET_HEADS, HEAD_DIM, HEAD_DIM), F32)
    else:
        s0 = layer_cache[0]
    q_r = rotary(heads(rq), pos, HEAD_DIM, RET_THETA)
    k_r = rotary(heads(rk), pos, HEAD_DIM, RET_THETA) * (HEAD_DIM ** -0.5)
    ro, ret_new = retention(q_r, k_r, heads(rv), s0)
    y_ret = layer_norm(ro, ret_gn_g.reshape(RET_HEADS, HEAD_DIM)).reshape(B, T, RET_W) * jax.nn.silu(rg.astype(F32))

    q_b = rotary(heads(sq), pos, ROPE_DIM, ROPE_THETA)
    k_b = rotary(heads(sk), pos, ROPE_DIM, ROPE_THETA)
    v_b = heads(sv).astype(F32)
    if layer_cache is None:
        y_swa = dilated_attention(q_b, k_b, v_b, None, None)
        keep = min(SWA_WINDOW, T)
        k_new, v_new = k_b[:, T - keep:], v_b[:, T - keep:]
    else:
        y_swa = dilated_attention(q_b, k_b, v_b, layer_cache[1], layer_cache[2])
        k_new, v_new = k_b, v_b

    conv_buf = None if layer_cache is None else layer_cache[3]
    y_conv, glu = conv_module(conv_in, conv_buf, conv_w, conv_b, conv_ln_g, conv_ln_b)
    conv_new = glu[:, T - (CONV_WIDTH - 1):] if layer_cache is None else glu

    y_sgu, v_rows = spatial_gating(sgu_in, sgu_ln_g, sgu_ln_b, sgu_w, sgu_b)

    y = jnp.concatenate([y_ret, y_swa.reshape(B, T, SWA_W), y_conv, y_sgu], axis=-1) @ w_out.astype(F32)
    if layer_cache is None:
        return y, (ret_new, k_new, v_new, conv_new)
    return y, (ret_new, k_new, v_new, conv_new, v_rows)

def trunk(x, pos, weights, cache):
    (w_in, w_out, ret_gn_g, conv_w, conv_b, conv_ln_g, conv_ln_b, sgu_ln_g, sgu_ln_b, sgu_w, sgu_b,
     ln1_g, ln1_b, ln2_g, ln2_b, rg_w, rg_b, re_w, re_b, w1, w3, w2) = weights
    collected = None
    for l in range(DEPTH):
        layer_cache = None if cache is None else (cache[0][l], cache[1][l], cache[2][l], cache[3][l])
        y, st = token_mixers(x, pos, w_in[l], w_out[l], ret_gn_g[l], conv_w[l], conv_b[l], conv_ln_g[l],
                             conv_ln_b[l], sgu_ln_g[l], sgu_ln_b[l], sgu_w[l], sgu_b[l], layer_cache)
        x = layer_norm(DN_ALPHA * x.astype(F32) + y, ln1_g[l], ln1_b[l]).astype(x.dtype)
        f = hier_moe(x, rg_w[l], rg_b[l], re_w[l], re_b[l], w1[l], w3[l], w2[l])
        x = layer_norm(DN_ALPHA * x.astype(F32) + f, ln2_g[l], ln2_b[l]).astype(x.dtype)
        if collected is None:
            collected = [[] for _ in st]
        for lst, s in zip(collected, st):
            lst.append(s)
    return x, [jnp.stack(lst) for lst in collected]

def setup_inputs(seed: int = 0) -> dict:
    key = jax.random.key(seed)
    k = jax.random.split(key, 28)

    def nrm(i, shape, scale):
        return jax.random.normal(k[i], shape, F32) * scale

    win = min(SWA_WINDOW, PAST_LEN)
    return {
        'x_prompt': nrm(0, (BATCH, SEQ, D_MODEL), 1.0),
        'x_sample': nrm(1, (DEC_BATCH, DEC_SEQ, D_MODEL), 1.0),
        'state_ret': nrm(2, (DEPTH, DEC_BATCH, RET_HEADS, HEAD_DIM, HEAD_DIM), 0.5),
        'cache_swa_k': nrm(3, (DEPTH, DEC_BATCH, win, SWA_HEADS, HEAD_DIM), 1.0),
        'cache_swa_v': nrm(4, (DEPTH, DEC_BATCH, win, SWA_HEADS, HEAD_DIM), 1.0),
        'state_conv': nrm(5, (DEPTH, DEC_BATCH, CONV_WIDTH - 1, CONV_CH), 0.5),
        'w_in': nrm(6, (DEPTH, D_MODEL, IN_W), D_MODEL ** -0.5),
        'w_out': nrm(7, (DEPTH, MIX_W, D_MODEL), DN_BETA * MIX_W ** -0.5),
        'ret_gn_g': 1.0 + nrm(8, (DEPTH, RET_W), 0.02),
        'conv_w': nrm(9, (DEPTH, CONV_WIDTH, CONV_CH), CONV_WIDTH ** -0.5),
        'conv_b': nrm(10, (DEPTH, CONV_CH), 0.02),
        'conv_ln_g': 1.0 + nrm(11, (DEPTH, CONV_CH), 0.02),
        'conv_ln_b': nrm(12, (DEPTH, CONV_CH), 0.02),
        'sgu_ln_g': 1.0 + nrm(13, (DEPTH, SGU_W), 0.02),
        'sgu_ln_b': nrm(14, (DEPTH, SGU_W), 0.02),
        'sgu_w': nrm(15, (DEPTH, SGU_GROUPS, SGU_CHUNK, SGU_CHUNK), SGU_CHUNK ** -0.5),
        'sgu_b': 1.0 + nrm(16, (DEPTH, SGU_GROUPS, SGU_CHUNK), 0.02),
        'ln1_g': 1.0 + nrm(17, (DEPTH, D_MODEL), 0.02),
        'ln1_b': nrm(18, (DEPTH, D_MODEL), 0.02),
        'ln2_g': 1.0 + nrm(19, (DEPTH, D_MODEL), 0.02),
        'ln2_b': nrm(20, (DEPTH, D_MODEL), 0.02),
        'router_g_w': nrm(21, (DEPTH, D_MODEL, N_GROUPS), D_MODEL ** -0.5),
        'router_g_b': nrm(22, (DEPTH, N_GROUPS), 0.01),
        'router_e_w': nrm(23, (DEPTH, N_GROUPS, D_MODEL, EXPERTS_PER_GROUP), D_MODEL ** -0.5),
        'router_e_b': nrm(24, (DEPTH, N_GROUPS, EXPERTS_PER_GROUP), 0.01),
        'moe_w1': nrm(25, (DEPTH, N_EXPERTS, D_MODEL, D_EXPERT), D_MODEL ** -0.5),
        'moe_w3': nrm(26, (DEPTH, N_EXPERTS, D_MODEL, D_EXPERT), D_MODEL ** -0.5),
        'moe_w2': nrm(27, (DEPTH, N_EXPERTS, D_EXPERT, D_MODEL), DN_BETA * D_EXPERT ** -0.5),
    }

def reference(x_prompt, x_sample, state_ret, cache_swa_k, cache_swa_v, state_conv,
              w_in, w_out, ret_gn_g, conv_w, conv_b, conv_ln_g, conv_ln_b,
              sgu_ln_g, sgu_ln_b, sgu_w, sgu_b, ln1_g, ln1_b, ln2_g, ln2_b,
              router_g_w, router_g_b, router_e_w, router_e_b, moe_w1, moe_w3, moe_w2):
    weights = (w_in, w_out, ret_gn_g, conv_w, conv_b, conv_ln_g, conv_ln_b, sgu_ln_g, sgu_ln_b, sgu_w, sgu_b,
               ln1_g, ln1_b, ln2_g, ln2_b, router_g_w, router_g_b, router_e_w, router_e_b, moe_w1, moe_w3, moe_w2)
    pos_prompt = jnp.arange(x_prompt.shape[1], dtype=jnp.int32)
    pos_sample = PAST_LEN + jnp.arange(x_sample.shape[1], dtype=jnp.int32)
    y_prompt, st_p = trunk(x_prompt, pos_prompt, weights, None)
    y_sample, st_s = trunk(x_sample, pos_sample, weights, (state_ret, cache_swa_k, cache_swa_v, state_conv))
    p_ret, p_k, p_v, p_conv = st_p
    s_ret, s_k, s_v, s_conv, s_sgu = st_s
    return (y_prompt, y_sample, p_ret, p_k, p_v, p_conv, s_ret, s_k, s_v, s_conv, s_sgu)


_drawn_inputs = setup_inputs


def setup_inputs(seed=0):
    import zlib

    import numpy as np

    out = dict(_drawn_inputs(seed))
    spreads = {}
    factors = {'ret_gn_g': 20.405,
     'conv_b': 2.806,
     'conv_ln_g': 29.194,
     'conv_ln_b': 27.784,
     'sgu_ln_g': 23.035,
     'sgu_ln_b': 24.414,
     'sgu_b': 20.306,
     'router_g_b': 5.469,
     'router_e_b': 9.819,
     'cache_swa_k': 4.664,
     'cache_swa_v': 3.218}
    for name, (base, spread) in spreads.items():
        noise = np.random.default_rng([zlib.crc32(name.encode()), seed]).standard_normal(out[name].shape)
        drawn = base * np.exp(spread * noise) if base else spread * noise
        out[name] = jnp.asarray(drawn.astype(out[name].dtype))
    for name, factor in factors.items():
        out[name] = (out[name] * factor).astype(out[name].dtype)
    return out
```

```python
from contextlib import ExitStack

import numpy as np
import concourse.bass as bass
from concourse import mybir

F32 = mybir.dt.float32
I32 = mybir.dt.int32
ALU = mybir.AluOpType
ACT = mybir.ActivationFunctionType
AX = mybir.AxisListType.X

D = 1024
SEQ = 512
DEPTH = 2
NB = 8
NT = 4
NS = NB * NT
PAST = 1024
HD = 64
NH = 4
NTOK = SEQ + NS
TILES = 5
ROWS = [128, 128, 128, 128, NS]
KT = D // 128
CW = 256
NCH = 11
NOUT = 4
TAPS = 31
PAD = TAPS - 1
CTXW = PAD + SEQ + NB * (PAD + NT)
ACCW = CTXW - PAD
SAMP0 = PAD + SEQ
NG, EPG, NE = 4, 8, 32
FF = 512
BLK = 128
MAXCNT = NTOK
NOVER = (2 * NTOK) // BLK
NI = (NE + NOVER + 1) // 2 * 2
ALPHA = float((2 * DEPTH) ** 0.25)
EPS = 1e-5
NEG = -1e30
SCALE = HD ** -0.5
NKEY = 640
DIL = ((128, 1), (512, 4), (2048, 16))
VAL, GATE, U, V, RG, RQ, RK, RV, SQ, SK, SV = range(NCH)


def multiplicity(dist):
    m = np.zeros(dist.shape)
    for window, dil in DIL:
        m += (dist >= 0) & (dist <= window) & (dist % dil == 0)
    return np.where(m > 0, np.log(np.maximum(m, 1)), NEG)


def shape_constants():
    p = np.arange(128)
    row_b, row_t = p // NT, p % NT
    g = 1.0 - 2.0 ** (-5.0 - np.arange(NH))
    parts = []

    def put(name, a):
        a = np.asarray(a, np.float64).reshape(a.shape[0], -1)
        full = np.zeros((128, a.shape[1]))
        full[: a.shape[0]] = a
        parts.append((name, full))

    put("ident", np.eye(128))
    put("attn_bias", multiplicity(384 + p[:, None] - np.arange(512)[None]))
    k = np.arange(NKEY - 512)
    idx = np.concatenate([np.arange(512, 1024), 16 * (k // 4) + k % 4, PAST + np.tile(np.arange(NT), NB)])
    owner = np.concatenate([np.full(NKEY, -1), np.repeat(np.arange(NB), NT)])
    rb, rt = p // 16, p % 4
    bias = multiplicity(PAST + rt[:, None] - idx[None])
    put("sample_bias", np.where((owner[None] >= 0) & (owner[None] != rb[:, None]), NEG, bias))
    causal = (p[None, :] >= p[:, None]).astype(float)
    put("ret_mask", causal[:, None, :] * (g[None, :] ** -(p[:, None] + 1.0))[:, :, None])
    s = np.arange(NS)
    same = (s[:, None] // NT == s[None] // NT) & (s[None] % NT >= s[:, None] % NT)
    put("ret_mask_s", same[:, None, :] * (g[None, :] ** -(s[:, None] % NT + 1.0))[:, :, None])
    step = np.stack([p] * 4 + [row_t], 1)
    length = np.array([128] * 4 + [NT])
    put("q_decay", g[None, None] ** (step[:, :, None] + 1.0))
    put("k_decay", g[None, None] ** np.maximum(length[None, :, None] - 1.0 - step[:, :, None], 0))
    head = 2 * np.arange(2)[None] + (p // 64)[:, None]
    put("c_decay", g[head] ** 128.0)
    put("c_decay_s", g[head] ** float(NT))
    pos = np.stack([128 * t + p for t in range(4)] + [np.where(p < NS, PAST + row_t, 0)], 1).astype(np.float32)
    for name, theta, rot in (("r", 10000.0, HD), ("s", 500000.0, HD // 4)):
        inv = np.float32(theta) ** (-np.arange(rot // 2, dtype=np.float32) * np.float32(2.0 / rot))
        ang = (pos[:, :, None] * inv[None, None]).astype(np.float32).astype(np.float64)
        put(name + "cos", np.cos(ang))
        put(name + "sin", np.sin(ang))
        if name == "r":
            put("kcos", np.cos(ang) * SCALE)
            put("ksin", np.sin(ang) * SCALE)
    put("sgu_mask", causal)
    put("sgu_mask_s", same.astype(float))
    put("own", (s[:, None] // NT == np.arange(NB)[None]).astype(float))
    put("before", (p[:, None] < p[None, :]).astype(float))
    put("ones", np.ones((128, 128)))
    put("iota", np.tile(np.arange(128), (128, 1)))
    put("first4", np.tile(4.0 - np.arange(4), (128, 1)))
    put("first8", np.tile(8.0 - np.arange(8), (128, 1)))
    tok = 128 * np.arange(TILES)[None] + p[:, None]
    put("tok", np.where(tok < NTOK, tok, 0))
    put("valid", (tok < NTOK).astype(float))
    at, where = {}, 0
    for name, a in parts:
        at[name] = (where, a.shape[1])
        where += a.shape[1]
    return np.concatenate([a for _, a in parts], 1).astype(np.float32), at


ROWPAR = [("ret_gn_g", 256), ("conv_ln_g", 256), ("conv_ln_b", 256), ("sgu_ln_g", 256), ("sgu_ln_b", 256),
          ("ln1_g", D), ("ln1_b", D), ("ln2_g", D), ("ln2_b", D), ("router_g_b", NG), ("router_e_b", NE)]
COLPAR = [("conv_w", 2 * TAPS), ("conv_b", 2), ("sgu_wT", 4 * 128), ("sgu_wT_s", 4 * NS), ("sgu_b", 4),
          ("sgu_b_s", 4), ("router_w", KT * (NG + NE)), ("conv_state", 2 * NB * PAD), ("ret_state", 2 * NB * HD)]


def offsets(fields):
    at, where = {}, 0
    for name, n in fields:
        at[name] = (where, n)
        where += n
    return at, where


PER = dict(par_in=32, xT_tr=30, xT_act=15, xT_dve=15, proj=55, proj_out=55,
           glu=1, ctx_tr=3, ctx_out=3, ctx_pool=1, conv_done=2, conv_tr=5, conv_out=5, conv_norm=1, conv_y=1,
           sgu_w=1, sgu_vn=1, sgu_z=3, sgu_y=1, rot_r=1, rot_s=1, qk_tr=9, qk_act=5, qk_dve=4, k_dec=1,
           ret_s=5, ret_a=5, ret_o=4, ret_upd=4, smp_o1=1, smp_o1c=1, vexp=1, smp_o=1, smp_upd=1, ret_y=1, 
           att_s=16, att_m=16, att_p=16, att_t=16, att_pT=16, att_o=16, att_y=16,
           qb_ok=1, kv_used=16, smp_m=1, smp_p=1, smp_n=1, smp_t=1, smp_pT=1, smp_oT=1,
           smp_back=1, smp_y=1, stores=16 * 9, wout=20, wout_out=20, x1=5, x1_store=80, x1_stat=1, x1_pow=1,
           logits=1, ex_in=1, ex_out=1, ex2_in=1, ex2_out=1, member=1, counts=1, onehot=1, idx_ps=1,
           routed=1, x2_stat=5, x2_pow=5, x2=5,
           st_in=3, st_out=3)


def trunk_program(nc, io, const_at):
    made = {}
    row_at, row_n = offsets(ROWPAR)
    col_at, col_n = offsets(COLPAR)
    ctx = ExitStack()
    with ctx:
        def sb(name, shape, dt=F32):
            return ctx.enter_context(nc.sbuf_tensor(name, shape, dt))[:]

        sems = {}

        def sem(name):
            if name not in sems:
                sems[name] = ctx.enter_context(nc.semaphore(name))
            return sems[name]

        x = sb("x", [128, TILES, D])
        xT = sb("xT", [128, KT, NTOK])
        const = sb("const", [128, sum(n for _, n in const_at.values())])
        rowpar = sb("rowpar", [128, row_n])
        colpar = sb("colpar", [128, col_n])
        small = sb("small", [128, 64])
        trip = sb("trip", [1, 2], I32)
        cum = sb("cum", [1, 2])
        items = sb("items", [1, NI], I32)
        slots = sb("slots", [128, 2, TILES], I32)
        gates = sb("gates", [128, 2, TILES])
        sidx = sb("sidx", [128, NI], I32)
        pstat = sb("pstat", [128, 2 * 4 * TILES])
        mv = sb("mv", [128, TILES, 4])
        bn = sb("bn", [128, TILES, 2, 6])
        halfc = sb("halfc", [128, 4 * TILES])

        def C(name):
            a, n = const_at[name]
            return const[:, a:a + n]

        def RP(name):
            a, n = row_at[name]
            return rowpar[:, a:a + n]

        def CP(name):
            a, n = col_at[name]
            return colpar[:, a:a + n]

        HCOLS = NCH * TILES * CW
        WCOLS = 4096
        ARENA = 31904
        arena = sb("arena", [128, ARENA])
        cursor = [0]

        def carve(n):
            a = cursor[0]
            cursor[0] += n
            assert cursor[0] <= ARENA, (cursor[0], ARENA)
            return arena[:, a:a + n]

        h = carve(HCOLS).rearrange("p (s t c) -> p s t c", s=NCH, t=TILES)
        ring = [carve(KT * CW).rearrange("p (k c) -> p k c", k=KT) for _ in range(2)]
        NKV = 3
        kv = [carve(2 * NKEY) for _ in range(NKV)]
        ctx_acc = carve(2 * CTXW + 2 * ACCW)
        ctxb = ctx_acc[:, 0:2 * CTXW].rearrange("p (c w) -> p c w", c=2)
        acc = ctx_acc[:, 2 * CTXW:2 * CTXW + 2 * ACCW].rearrange("p (c w) -> p c w", c=2)
        vexp = ctx_acc[0:NS, 0:NH * NB * HD].rearrange("p (h b e) -> p h b e", h=NH, b=NB)
        ret_S = carve(2 * HD).rearrange("p (c e) -> p c e", c=2)
        sm = [carve(512) for _ in range(2)]
        pT = [carve(512) for _ in range(2)]
        ss = carve(672)
        PTs = carve(6 * 128).rearrange("p (k r) -> p k r", k=6)
        QB = carve(2 * NB * 32).rearrange("p (c q) -> p c q", c=2)
        scr = carve(TILES * CW)
        pscr = carve(TILES * CW)
        cursor[0] = 0
        w13 = [[None, None], [None, None]]
        w2 = [None, None]
        for q in range(2):
            for j in range(2):
                w13[q][j] = carve(WCOLS).rearrange("p (c f) -> p c f", c=KT)
            w2[q] = carve(WCOLS).rearrange("p (c n) -> p c n", c=4)
        assert 3 * WCOLS <= HCOLS
        ygot = [[arena[:, (2 * q + j) * D:(2 * q + j + 1) * D] for j in range(2)] for q in range(2)]
        xg = [carve(D) for _ in range(2)]
        yo = [carve(D) for _ in range(2)]
        gidx = [carve(1).bitcast(I32) for _ in range(2)]
        flat = xT[:].rearrange("p k n -> p (k n)")
        xgT = [flat[:, q * D:(q + 1) * D].rearrange("p (c m) -> p c m", c=KT) for q in range(2)]
        hm = [flat[:, 2 * D + q * FF:2 * D + (q + 1) * FF] for q in range(2)]
        sg = hm
        hT = [flat[:, 2 * D + (2 + q) * FF:2 * D + (3 + q) * FF].rearrange("p (c m) -> p c m", c=4) for q in range(2)]
        cursor[0] = HCOLS
        R = carve(6144)

        ps = [ctx.enter_context(nc.psum_tensor(f"ps{i}", [128, 512], F32)) for i in range(8)]

        x1d = io["x1d"]
        yd = io["yd"]

        def onehots(R):
            a = 2048
            place = R[:, a:a + 2 * TILES * 128].rearrange("p (k m) -> p k m", k=2 * TILES)
            b = a + 2 * TILES * 128
            whose = R[:, b:b + 2 * TILES * NI].rearrange("p (k m) -> p k m", k=2 * TILES)
            return place, whose

        class Eng:

            def __init__(self, eng, chain):
                self.e, self.chain, self.n, self.L = eng, chain, 0, 0

            def need(self, name, n):
                assert 0 < n <= PER[name], (name, n)
                self.e.wait_ge(sem(name), self.L * PER[name] + n)

            def done(self, ins, name, by=1):
                made[name] = made.get(name, 0) + by
                ins.then_inc(sem(name), by)
                return ins

            def link(self, ins):
                self.n += 1
                ins.then_inc(sem(self.chain + "_chain"), 1)
                self.e.wait_ge(sem(self.chain + "_chain"), self.n)

        start_sem = sem("start")
        block = ctx.enter_context(nc.Block())

        @block.sync
        def _(sp):
            E = Eng(sp, "none")
            sp.dma_start(const[:], io["const"]).then_inc(start_sem, 16)
            for t in range(TILES):
                sp.dma_start(x[0:ROWS[t], t, :], io["x_in"][128 * t:128 * t + ROWS[t], :]).then_inc(start_sem, 16)
            for L in range(DEPTH):
                E.L = L
                sp.wait_ge(sem("x2"), L * TILES)
                E.done(sp.dma_start(rowpar[:], io["rowpar"][bass.ds(L * 128, 128), :]), "par_in", 16)
                E.done(sp.dma_start(colpar[:], io["colpar"][bass.ds(L * 128, 128), :]), "par_in", 16)

                def ring_load(c):
                    if c >= 2:
                        E.need("proj" if c - 2 < NCH else "wout", (c - 1 if c - 2 < NCH else c - 1 - NCH) * TILES)
                    src = io["w_proj"][bass.ds(L * (NCH + NOUT) + c, 1), :, :].rearrange("a p n -> (a p) n")
                    sp.dma_start(ring[c % 2].rearrange("p k c -> p (k c)"), src).then_inc(sem(f"ring{c % 2}"), 16)

                def kv_load(i):
                    if i >= NKV:
                        E.need("kv_used", i - NKV + 1)
                    src = io["kv"][bass.ds(L * 16 + i, 1), :, :].rearrange("a p n -> (a p) n")
                    sp.dma_start(kv[i % NKV], src).then_inc(sem(f"kv{i % NKV}"), 16)

                for c in range(NCH):
                    ring_load(c)
                    if c < NKV:
                        kv_load(c)
                for c in range(NCH, NCH + 2):
                    ring_load(c)
                for i in range(NKV, 16):
                    kv_load(i)
                E.need("glu", 1)
                out = io["p_conv"][bass.ds(L, 1)].rearrange("a p c -> (a p) c")
                E.done(sp.dma_start(out, h[128 - PAD:128, VAL, 3, :]), "stores", 16)
                out = io["s_conv"][bass.ds(L, 1)].rearrange("a p c -> (a p) c")
                E.done(sp.dma_start(out, h[0:NS, VAL, 4, :]), "stores", 16)
                E.need("sgu_vn", 1)
                out = io["s_sgu"][bass.ds(L, 1)].rearrange("a p c -> (a p) c")
                E.done(sp.dma_start(out, h[0:NS, V, 4, :]), "stores", 16)
                E.need("rot_s", 1)
                E.need("proj_out", 55)
                for name, s in (("k", SK), ("v", SV)):
                    out = io["p_" + name][bass.ds(L, 1)].rearrange("a (t p) c -> p (a t) c", p=128)
                    E.done(sp.dma_start(out, h[:, s, 0:4, :]), "stores", 16)
                out = io["s_k"][bass.ds(L, 1)].rearrange("a p c -> (a p) c")
                E.done(sp.dma_start(out, h[0:NS, SK, 4, :]), "stores", 16)
                out = io["s_v"][bass.ds(L, 1)].rearrange("a p c -> (a p) c")
                E.done(sp.dma_start(out, h[0:NS, SV, 4, :]), "stores", 16)
                E.need("ret_upd", 4)
                out = io["p_ret"][bass.ds(L, 1)].rearrange("a p n -> (a p) n")
                E.done(sp.dma_start(out, ret_S.rearrange("p c e -> p (c e)")), "stores", 16)
                E.need("smp_upd", 1)
                out = io["s_ret"][bass.ds(L, 1)].rearrange("a p n -> (a p) n")
                E.done(sp.dma_start(out, CP("ret_state")), "stores", 16)
                for c in range(NCH + 2, NCH + NOUT):
                    ring_load(c)
                E.need("stores", 16 * 9)
                E.need("xT_tr", 20)
                E.need("smp_back", 1)
                def expert_load(j, q, i, e):
                    src = io[("w1", "w3", "w2")[j]][bass.ds(L * NE + e, 1), :, :].rearrange("a p n -> (a p) n")
                    dst = (w13[q][j] if j < 2 else w2[q]).rearrange("p c n -> p (c n)")
                    sp.dma_start(dst, src).then_inc(sem(f"w{j}_{q}"), 16)

                for j in range(3):
                    expert_load(j, 0, None, 0)
                for t in range(TILES):
                    E.need("x1", t + 1)
                    E.done(sp.dma_start(x1d[128 * t:128 * t + ROWS[t], :], x[0:ROWS[t], t, :]), "x1_store", 16)
                E.need("routed", 1)
                for j in range(3):
                    expert_load(j, 1, None, 1)
                lo = sp.value_load(trip[0:1, 0:1], min_val=1, max_val=1 + (DEPTH - 1) * NI // 2)
                turns = sp.value_load(trip[0:1, 1:2], min_val=NE // 2, max_val=NI // 2)

                used = (("w0_used", "w1_used", "y1_ps")[j] for j in range(3))
                used = list(used)
                with sp.Fori(1, turns) as turn:
                    i = sp.snap(lo + turn)
                    ea = sp.value_load(items[0:1, bass.ds(turn * 2, 1)], min_val=0, max_val=NE - 1)
                    eb = sp.value_load(items[0:1, bass.ds(turn * 2 + 1, 1)], min_val=0, max_val=NE - 1)
                    ra = sp.snap((ea + L * NE))
                    rb = sp.snap((eb + L * NE))
                    for j, q in ((0, 0), (1, 0), (0, 1), (1, 1), (2, 0), (2, 1)):
                        src = io[("w1", "w3", "w2")[j]][bass.ds((ra, rb)[q], 1), :, :].rearrange("a p n -> (a p) n")
                        dst = (w13[q][j] if j < 2 else w2[q]).rearrange("p c n -> p (c n)")
                        sp.wait_ge(sem(f"{used[j]}{q}"), i)
                        sp.dma_start(dst, src).then_inc(sem(f"w{j}_{q}"), 16)
                    for q in range(2):
                        row = sp.snap((turn - 1) * (2 * BLK) + q * BLK)
                        sp.wait_ge(sem(f"y_act{q}"), i)
                        sp.wait_ge(sem(f"y_dve{q}"), i)
                        sp.dma_start(yd[bass.ds(row, BLK), :], yo[q]).then_inc(sem(f"y_stored{q}"), 16)
                for q in range(2):
                    row = sp.snap((turns - 1) * (2 * BLK) + q * BLK)
                    sp.wait_ge(sem(f"y_act{q}"), lo + turns)
                    sp.wait_ge(sem(f"y_dve{q}"), lo + turns)
                    sp.dma_start(yd[bass.ds(row, BLK), :], yo[q]).then_inc(sem(f"y_stored{q}"), 16)
            for t in range(TILES):
                sp.wait_ge(sem("x2"), (DEPTH - 1) * PER["x2"] + t + 1)
                sp.dma_start(io["y"][128 * t:128 * t + ROWS[t], :], x[0:ROWS[t], t, :]).then_inc(sem("y_out"), 16)
            sp.wait_ge(sem("y_out"), 16 * TILES)

        @block.tensor
        def _(pe):
            E = Eng(pe, "none")
            ident = C("ident")
            pe.wait_ge(start_sem, 16 * (1 + TILES))
            for L in range(DEPTH):
                E.L = L
                turned = [0]

                def turn_rows(source):
                    for t in range(TILES):
                        n = ROWS[t]
                        for g in range(2):
                            k = turned[0]
                            if k >= 2:
                                E.need(("xT_act", "xT_dve")[g], k // 2)
                            for j in range(4):
                                ins = pe.transpose(ps[g][:, j * 128:j * 128 + n], source(t, 4 * g + j), ident[0:n, 0:n])
                            E.done(ins, "xT_tr")
                            turned[0] += 1

                def x_block(t, k):
                    return x[0:ROWS[t], t, k * 128:(k + 1) * 128]

                pe.wait_ge(sem("x2"), L * TILES)
                turn_rows(x_block)

                def chunk(c, done, left):
                    pe.wait_ge(sem(f"ring{c % 2}"), (L * (8 - c % 2) + c // 2 + 1) * 16)
                    for t in range(TILES):
                        n = ROWS[t]
                        j = (c if c < NCH else c - NCH) * TILES + t
                        if j >= TILES:
                            E.need(left, j - TILES + 1)
                        for k in range(KT):
                            ins = pe.matmul(ps[2 + t][0:n, 0:CW], xT[:, k, 128 * t:128 * t + n], ring[c % 2][:, k, :],
                                            start=(k == 0), stop=(k == KT - 1))
                        E.done(ins, done)

                E.need("xT_act", 5)
                E.need("xT_dve", 5)
                for c in range(5):
                    chunk(c, "proj", "proj_out")
                E.need("glu", 1)
                for cb in range(2):
                    for t in range(4):
                        ins = pe.transpose(ps[cb][:, t * 128:(t + 1) * 128], h[:, VAL, t, cb * 128:(cb + 1) * 128], ident)
                    E.done(ins, "ctx_tr")
                E.need("ctx_out", 1)
                for cb in range(2):
                    ins = pe.transpose(ps[0][:, cb * NS:(cb + 1) * NS], h[0:NS, VAL, 4, cb * 128:(cb + 1) * 128],
                                       ident[0:NS, 0:NS])
                E.done(ins, "ctx_tr")
                for c in range(5, NCH):
                    chunk(c, "proj", "proj_out")
                E.need("conv_done", 2)
                E.need("ctx_out", 3)
                for t in range(TILES):
                    n = ROWS[t]
                    if t >= 2:
                        E.need("conv_out", t - 1)
                    for cb in range(2):
                        src = acc[:, cb, 128 * t:128 * t + 128] if t < 4 else scr[:, cb * NS:(cb + 1) * NS]
                        ins = pe.transpose(ps[t % 2][0:n, cb * 128:(cb + 1) * 128], src, ident)
                    E.done(ins, "conv_tr")
                E.need("sgu_vn", 1)
                E.need("sgu_w", 1)
                wT = CP("sgu_wT").rearrange("p (g t) -> p g t", g=4)
                wTs = CP("sgu_wT_s").rearrange("p (g t) -> p g t", g=4)
                E.need("proj_out", 55)
                for g in range(4):
                    ins = pe.matmul(ps[6 + g // 2][:, (g % 2) * 256:(g % 2) * 256 + 256], wT[:, g, :],
                                    h[:, V, 0:4, g * 64:(g + 1) * 64], start=True, stop=True)
                    if g % 2:
                        E.done(ins, "sgu_z")
                for g in range(4):
                    ins = pe.matmul(ps[5][0:NS, g * 64:(g + 1) * 64], wTs[0:NS, g, :], h[0:NS, V, 4, g * 64:(g + 1) * 64],
                                    start=True, stop=True)
                E.done(ins, "sgu_z")
                E.need("rot_r", 1)
                E.need("rot_s", 1)
                E.need("conv_out", 5)
                order = [(s, hp) for s in (RQ, RK, SQ, SK) for hp in range(2)]
                for k, (s, hp) in enumerate(order):
                    if k >= 2:
                        E.need(("qk_act", "qk_dve")[k % 2], k // 2)
                    for t in range(4):
                        ins = pe.transpose(ps[k % 2][:, t * 128:(t + 1) * 128], h[:, s, t, hp * 128:(hp + 1) * 128], ident)
                    E.done(ins, "qk_tr")
                E.need("qk_act", 4)
                for k, (s, hp) in enumerate(order):
                    ins = pe.transpose(ps[0][:, k * NS:(k + 1) * NS], h[0:NS, s, 4, hp * 128:(hp + 1) * 128],
                                       ident[0:NS, 0:NS])
                E.done(ins, "qk_tr")
                E.need("qk_act", 5)
                E.need("qk_dve", 4)
                E.need("sgu_y", 1)

                def half(hh):
                    return slice(64 * hh, 64 * hh + 64)

                def ret_scores(n):
                    if n >= 2:
                        E.need("ret_a", n - 1)
                    for hd in range(NH):
                        hp, hh = hd // 2, hd % 2
                        b = ps[((2, 5), (6, 7))[n % 2][hh]]
                        ins = pe.matmul(b[:, hp * 128:(hp + 1) * 128], xT[half(hh), 2 + hp, n * 128:(n + 1) * 128],
                                        xT[half(hh), hp, n * 128:(n + 1) * 128], start=True, stop=True)
                    E.done(ins, "ret_s")

                ret_scores(0)
                E.need("k_dec", 1)
                for n in range(4):
                    if n < 3:
                        ret_scores(n + 1)
                    E.need("ret_a", n + 1)
                    if n:
                        E.need("ret_upd", n)
                    for hd in range(NH):
                        hp, hh = hd // 2, hd % 2
                        o = ps[(3, 1)[hh]][:, hp * HD:(hp + 1) * HD]
                        pe.matmul(o, pT[n % 2][:, hd * 128:(hd + 1) * 128],
                                  h[:, RV, n, hd * HD:(hd + 1) * HD], start=True, stop=(n == 0))
                        if n:
                            pe.matmul(o, xT[half(hh), hp, n * 128:(n + 1) * 128],
                                      ret_S[half(hh), hp, :], start=False, stop=True)
                    for hp in range(2):
                        ins = pe.matmul(ps[4][:, hp * 128:(hp + 1) * 128], h[:, RK, n, hp * 128:(hp + 1) * 128],
                                        h[:, RV, n, hp * 128:(hp + 1) * 128], start=True, stop=True)
                    E.done(ins, "ret_o")
                s0 = CP("ret_state").rearrange("p (c b e) -> p c b e", c=2, b=NB)
                for hd in range(NH):
                    hp, hh = hd // 2, hd % 2
                    ins = pe.matmul(ps[(2, 5)[hh]][0:NS, hp * NS:(hp + 1) * NS], xT[half(hh), 2 + hp, SEQ:NTOK],
                                    xT[half(hh), hp, SEQ:NTOK], start=True, stop=True)
                E.done(ins, "ret_s")
                for hd in range(NH):
                    hp, hh = hd // 2, hd % 2
                    for b in range(NB):
                        ins = pe.matmul(ps[6 + hh][0:64, hp * NS + b * NT:hp * NS + (b + 1) * NT], s0[half(hh), hp, b, :],
                                        xT[half(hh), hp, SEQ + b * NT:SEQ + (b + 1) * NT], start=True, stop=True)
                E.done(ins, "smp_o1")
                E.need("ret_a", 5)
                E.need("smp_o1c", 1)
                E.need("ret_upd", 4)
                for hd in range(NH):
                    pe.matmul(ps[3][0:NS, hd * HD:(hd + 1) * HD], sm[0][0:NS, hd * NS:(hd + 1) * NS],
                              h[0:NS, RV, 4, hd * HD:(hd + 1) * HD], start=True, stop=False)
                    ins = pe.matmul(ps[3][0:NS, hd * HD:(hd + 1) * HD], sm[1][0:64, hd * NS:(hd + 1) * NS],
                                    ident[0:64, 0:64], start=False, stop=True)
                E.need("vexp", 1)
                for hd in range(NH):
                    hp, hh = hd // 2, hd % 2
                    ins = pe.matmul(ps[4 + hp][half(hh), :], h[0:NS, RK, 4, hd * HD:(hd + 1) * HD],
                                    vexp[:, hd, :, :].rearrange("p b e -> p (b e)"), start=True, stop=True)
                E.done(ins, "smp_o")

                def att_scores(u):
                    i, hd = u // 4, u % 4
                    hp, hh = hd // 2, hd % 2
                    b = ps[2] if u % 2 == 0 else ps[5]
                    if u >= 2:
                        E.need("att_m", u - 1)
                    n = (i + 1) * 128
                    ins = pe.matmul(b[:, 0:n], xT[half(hh), 4 + hp, i * 128:(i + 1) * 128], xT[half(hh), 6 + hp, 0:n],
                                    start=True, stop=True)
                    E.done(ins, "att_s")

                E.need("smp_upd", 1)
                att_scores(0)
                for u in range(16):
                    i, hd = u // 4, u % 4
                    if u < 15:
                        att_scores(u + 1)
                    E.need("att_p", u + 1)
                    if u >= 2:
                        E.need("att_pT", u - 1)
                        E.need("att_y", u - 1)
                    bt = ps[3] if u % 2 == 0 else ps[6]
                    bo = ps[4] if u % 2 == 0 else ps[7]
                    for k in range(i + 1):
                        ins = pe.transpose(bt[:, k * 128:(k + 1) * 128], sm[u % 2][:, k * 128:(k + 1) * 128], ident)
                    E.done(ins, "att_t")
                    E.need("att_pT", u + 1)
                    for k in range(i + 1):
                        ins = pe.matmul(bo[:, 0:HD], pT[u % 2][:, k * 128:(k + 1) * 128], h[:, SV, k, hd * HD:(hd + 1) * HD],
                                        start=(k == 0), stop=(k == i))
                    E.done(ins, "att_o")
                E.need("qb_ok", 1)
                E.need("att_m", 16)
                E.need("att_y", 16)
                seen = [0] * NKV

                def kv_wait(i):
                    uses = len(range(i % NKV, 16, NKV))
                    pe.wait_ge(sem(f"kv{i % NKV}"), (L * uses + i // NKV + 1) * 16)

                for b in range(NB):
                    kv_wait(b)
                    kb = kv[b % NKV].rearrange("p (c k) -> p c k", c=2)
                    rows = slice(32 * (b // 2), 32 * (b // 2) + 32)
                    for hp in range(2):
                        st, en = (b % 2 == 0 and hp == 0), (b % 2 == 1 and hp == 1)
                        q = QB[:, hp, 32 * b:32 * b + 32]
                        pos = (0, 32 * (b // 2))
                        pe.matmul(ps[0][rows, :], q, kb[:, hp, 0:512], start=st, stop=en, tile_position=pos)
                        pe.matmul(ps[1][rows, 0:128], q, kb[:, hp, 512:640], start=st, stop=en, tile_position=pos)
                        ins = pe.matmul(ps[2][rows, 0:NS], q, xT[:, 6 + hp, SEQ:NTOK], start=st, stop=en, tile_position=pos)
                    E.done(ins, "kv_used")
                E.need("smp_n", 1)
                E.need("att_pT", 16)
                for k in range(4):
                    pe.transpose(ps[3][:, k * 128:(k + 1) * 128], ss[:, k * 128:(k + 1) * 128], ident)
                pe.transpose(ps[5][:, 0:128], ss[:, 512:640], ident)
                ins = pe.transpose(ps[5][0:NS, 128:256], ss[:, 640:672], ident)
                E.done(ins, "smp_t")
                E.need("smp_pT", 1)
                for b in range(NB):
                    kv_wait(NB + b)
                    vb = kv[(NB + b) % NKV].rearrange("p (k c) -> p k c", k=5)
                    for hp in range(2):
                        o = ps[4][:, 16 * b + 8 * hp:16 * b + 8 * hp + 8]
                        for k in range(5):
                            pe.matmul(o, vb[:, k, hp * 128:(hp + 1) * 128], PTs[:, k, 16 * b + 8 * hp:16 * b + 8 * hp + 8],
                                      start=(k == 0), stop=False)
                        ins = pe.matmul(o, h[0:NS, SV, 4, hp * 128:(hp + 1) * 128],
                                        PTs[0:NS, 5, 16 * b + 8 * hp:16 * b + 8 * hp + 8], start=False, stop=True)
                    E.done(ins, "kv_used")
                E.need("smp_oT", 1)
                for hp in range(2):
                    ins = pe.transpose(ps[5][0:NS, hp * 128:(hp + 1) * 128], sm[0][:, hp * NS:(hp + 1) * NS], ident)
                E.done(ins, "smp_back")

                E.need("smp_y", 1)
                E.need("ret_y", 1)
                E.need("conv_y", 1)
                mix = [RQ, SQ, GATE, U]
                turn_rows(lambda t, k: h[0:ROWS[t], mix[k // 2], t, (k % 2) * 128:(k % 2) * 128 + 128])
                E.need("xT_act", 10)
                E.need("xT_dve", 10)
                for c in range(NCH, NCH + NOUT):
                    chunk(c, "wout", "wout_out")
                E.need("x1", 5)
                turn_rows(x_block)
                E.need("xT_act", 15)
                E.need("xT_dve", 15)
                E.need("wout_out", 20)
                rw = CP("router_w").rearrange("p (k n) -> p k n", k=KT)
                for t in range(TILES):
                    n = ROWS[t]
                    for k in range(KT):
                        ins = pe.matmul(ps[2][0:n, t * 36:t * 36 + 36], xT[:, k, 128 * t:128 * t + n], rw[:, k, :],
                                        start=(k == 0), stop=(k == KT - 1))
                E.done(ins, "logits")
                E.need("member", 1)
                memb = R[:, 0:TILES * NE].rearrange("p (t e) -> p t e", t=TILES)
                for t in range(TILES):
                    for t2 in range(t + 1):
                        pe.matmul(ps[3][:, t * NE:(t + 1) * NE], C("before") if t2 == t else C("ones"), memb[:, t2, :],
                                  start=(t2 == 0), stop=(t2 == t))
                for t2 in range(TILES):
                    ins = pe.matmul(ps[4][:, 0:NE], C("ones"), memb[:, t2, :], start=(t2 == 0), stop=(t2 == TILES - 1))
                E.done(ins, "counts")
                E.need("onehot", 1)
                place, whose = onehots(R)
                for k in range(2 * TILES):
                    ins = pe.matmul(ps[5][:, 0:NI], place[:, k, :], whose[:, k, :], start=(k == 0), stop=(k == 2 * TILES - 1))
                E.done(ins, "idx_ps")
                E.need("routed", 1)
                lo = pe.value_load(trip[0:1, 0:1], min_val=1, max_val=1 + (DEPTH - 1) * NI // 2)
                turns = pe.value_load(trip[0:1, 1:2], min_val=NE // 2, max_val=NI // 2)
                with pe.Fori(0, turns) as turn:
                    i = pe.snap(lo + turn)
                    for q in range(2):
                        pe.wait_ge(sem(f"xg{q}"), i * 16)
                        v = xg[q].rearrange("p (k c) -> p c k", c=KT)
                        for g in range(2):
                            if q:
                                pe.wait_ge(sem(("xgT_act0", "xgT_dve0")[g]), i + 1)
                            for c in range(4):
                                ins = pe.transpose(ps[g][:, c * BLK:(c + 1) * BLK], v[:, 4 * g + c, :], ident)
                            ins.then_inc(sem(f"xg_tr{g}_{q}"), 1)
                    for q in range(2):
                        pe.wait_ge(sem(f"xgT_act{q}"), i + 1)
                        pe.wait_ge(sem(f"xgT_dve{q}"), i + 1)
                        for j in range(2):
                            pe.wait_ge(sem(f"w{j}_{q}"), (i + 1) * 16)
                            pe.wait_ge(sem(f"hm{q}"), i)
                            for c in range(KT):
                                ins = pe.matmul(ps[2 + 2 * q + j][0:BLK, :], xgT[q][:, c, :], w13[q][j][:, c, :],
                                                start=(c == 0), stop=(c == KT - 1))
                            ins.then_inc(sem(f"w{j}_used{q}"), 1)
                    for q in range(2):
                        pe.wait_ge(sem(f"hm{q}"), i + 1)
                        v = hm[q].rearrange("p (f c) -> p c f", c=4)
                        for c in range(4):
                            ins = pe.transpose(ps[q][:, c * BLK:(c + 1) * BLK], v[:, c, :], ident)
                        ins.then_inc(sem(f"hm_tr{q}"), 1)
                        pe.wait_ge(sem(f"hT{q}"), i + 1)
                        pe.wait_ge(sem(f"w2_{q}"), (i + 1) * 16)
                        if q:
                            pe.wait_ge(sem("y_act0"), i + 1)
                            pe.wait_ge(sem("y_dve0"), i + 1)
                        else:
                            pe.wait_ge(sem("y_act1"), i)
                            pe.wait_ge(sem("y_dve1"), i)
                        for n in range(2):
                            for c in range(4):
                                ins = pe.matmul(ps[6 + n][0:BLK, :], hT[q][:, c, :], w2[q][:, c, n * 512:(n + 1) * 512],
                                                start=(c == 0), stop=(c == 3))
                            ins.then_inc(sem(f"y{n}_ps{q}"), 1)

        @block.scalar
        def _(act):
            E = Eng(act, "act")
            act.wait_ge(start_sem, 16 * (1 + TILES))
            act.wait_ge(sem("pinit"), 2)
            for L in range(DEPTH):
                E.L = L
                turned = [0]

                def turn_out():
                    for t in range(TILES):
                        n = ROWS[t]
                        E.need("xT_tr", 2 * turned[0] + 1)
                        src = ps[0][:, :].rearrange("p (j m) -> p j m", j=4)[:, :, 0:n]
                        E.done(act.copy(xT[:, 0:4, 128 * t:128 * t + n], src), "xT_act")
                        turned[0] += 1

                turn_out()
                func = {GATE: ACT.Sigmoid, U: ACT.Gelu_apprx_tanh, V: ACT.Gelu_apprx_tanh, RG: ACT.Silu}
                for c in range(NCH):
                    for t in range(TILES):
                        n = ROWS[t]
                        E.need("proj", c * TILES + t + 1)
                        E.done(act.activation(h[0:n, c, t, :], ps[2 + t][0:n, 0:CW], func.get(c, ACT.Copy)), "proj_out")
                E.need("conv_norm", 1)
                E.done(act.activation(h[:, GATE], h[:, GATE], ACT.Silu), "conv_y")
                for k in range(0, 8, 2):
                    E.need("qk_tr", k + 1)
                    E.done(act.copy(xT[:, k, 0:SEQ], ps[0][:, :]), "qk_act")
                E.need("qk_tr", 9)
                E.done(act.copy(xT[:, 0:8, SEQ:NTOK], ps[0][:, 0:8 * NS].rearrange("p (k n) -> p k n", k=8)), "qk_act")
                E.need("smp_o1", 1)
                for hh in range(2):
                    dst = sm[1][0:64, 0:NH * NS].rearrange("p (c g n) -> p c g n", c=2, g=2)[:, :, hh, :]
                    ins = act.copy(dst, ps[6 + hh][0:64, 0:2 * NS].rearrange("p (c n) -> p c n", c=2))
                E.done(ins, "smp_o1c")
                for u in range(16):
                    n = (u // 4 + 1) * 128
                    E.need("att_m", u + 1)
                    E.done(act.activation(sm[u % 2][:, 0:n], sm[u % 2][:, 0:n], ACT.Exp, bias=small[:, u % 2:u % 2 + 1],
                                          accum_out=small[:, 2 + u % 2:3 + u % 2]), "att_p")
                    E.need("att_t", u + 1)
                    if u >= 2:
                        E.need("att_o", u - 1)
                    bt = ps[3] if u % 2 == 0 else ps[6]
                    E.done(act.copy(pT[u % 2][:, 0:n], bt[:, 0:n]), "att_pT")
                E.need("smp_m", 1)
                E.done(act.activation(ss, ss, ACT.Exp, bias=small[:, 4:5], accum_out=small[:, 5:6]), "smp_p")
                E.need("smp_t", 1)
                E.link(act.copy(PTs[:, 0:4, :], ps[3][:, :].rearrange("p (k r) -> p k r", k=4)))
                E.link(act.copy(PTs[:, 4, :], ps[5][:, 0:128]))
                E.done(act.copy(PTs[0:NS, 5, :], ps[5][0:NS, 128:256]), "smp_pT")
                turn_out()
                turn_out()
                E.need("ex_in", 1)
                ex = R[:, 400:400 + TILES * NG]
                E.done(act.activation(ex, ex, ACT.Exp), "ex_out")
                E.need("ex2_in", 1)
                ex2 = R[:, 440:440 + TILES]
                E.done(act.activation(ex2, ex2, ACT.Exp), "ex2_out")
                E.need("routed", 1)
                lo = act.value_load(trip[0:1, 0:1], min_val=1, max_val=1 + (DEPTH - 1) * NI // 2)
                turns = act.value_load(trip[0:1, 1:2], min_val=NE // 2, max_val=NI // 2)
                with act.Fori(0, turns) as turn:
                    i = act.snap(lo + turn)
                    for q in range(2):
                        act.wait_ge(sem(f"xg_tr0_{q}"), i + 1)
                        act.copy(xgT[q][:, 0:4, :], ps[0][:, 0:4 * BLK].rearrange("p (c m) -> p c m", c=4))\
                           .then_inc(sem(f"xgT_act{q}"), 1)
                    for q in range(2):
                        act.wait_ge(sem(f"w0_used{q}"), i + 1)
                        act.activation(sg[q], ps[2 + 2 * q][0:BLK, :], ACT.Silu).then_inc(sem(f"sg{q}"), 1)
                    for q in range(2):
                        act.wait_ge(sem(f"hm_tr{q}"), i + 1)
                        act.copy(hT[q], ps[q][:, 0:4 * BLK].rearrange("p (c m) -> p c m", c=4)).then_inc(sem(f"hT{q}"), 1)
                        act.wait_ge(sem(f"y0_ps{q}"), i + 1)
                        act.wait_ge(sem(f"y_stored{q}"), i * 16)
                        act.copy(yo[q][:, 0:512], ps[6][0:BLK, :]).then_inc(sem(f"y_act{q}"), 1)

        @block.vector
        def _(dve):
            E = Eng(dve, "dve")
            v = nc.vector
            dve.memset(cum[:], 1.0).then_inc(sem("init"), 1)
            dve.wait_ge(sem("init"), 1)
            dve.wait_ge(start_sem, 16 * (1 + TILES))

            def group_norm(rows, groups, size, stat, gain, bias, out):
                n = TILES * groups
                r3 = rows.rearrange("p t (g c) -> p (t g) c", c=size)
                s3 = scr[:, 0:n * size].rearrange("p (a c) -> p a c", c=size)
                mean, var = stat[:, 0:n], stat[:, n:2 * n]
                E.link(dve.tensor_reduce(mean, r3, AX, ALU.add))
                E.link(dve.tensor_scalar(mean, mean, 1.0 / size, None, ALU.mult))
                E.link(dve.tensor_tensor(r3, r3, mean.unsqueeze(2).to_broadcast([128, n, size]), ALU.subtract))
                E.link(dve.tensor_tensor(s3, r3, r3, ALU.mult))
                E.link(dve.tensor_reduce(var, s3, AX, ALU.add))
                E.done(dve.tensor_scalar(var, var, 1.0 / size, EPS, ALU.mult, ALU.add), "st_in")
                stat_n[0] += 1
                E.need("st_out", stat_n[0])
                E.link(dve.tensor_tensor(r3, r3, var.unsqueeze(2).to_broadcast([128, n, size]), ALU.mult))
                g4 = gain.unsqueeze(1).to_broadcast([128, TILES, groups * size])
                ins = dve.tensor_tensor(out, rows, g4, ALU.mult)
                if bias is not None:
                    E.link(ins)
                    ins = dve.tensor_tensor(out, out, bias.unsqueeze(1).to_broadcast([128, TILES, groups * size]), ALU.add)
                return ins

            for L in range(DEPTH):
                E.L = L
                turned = [0]
                stat_n = [0]
                stats = pstat

                def turn_out():
                    for t in range(TILES):
                        n = ROWS[t]
                        E.need("xT_tr", 2 * turned[0] + 2)
                        src = ps[1][:, :].rearrange("p (j m) -> p j m", j=4)[:, :, 0:n]
                        E.done(dve.tensor_copy(xT[:, 4:8, 128 * t:128 * t + n], src), "xT_dve")
                        turned[0] += 1

                turn_out()
                E.need("ctx_pool", 1)
                for cb in range(2):
                    E.need("ctx_tr", cb + 1)
                    E.done(dve.tensor_copy(ctxb[:, cb, PAD:SAMP0], ps[cb][:, :]), "ctx_out")
                E.need("ctx_tr", 3)
                smp = ctxb[:, :, SAMP0:CTXW].rearrange("p c (b w) -> p c b w", b=NB)
                for cb in range(2):
                    src = ps[0][:, cb * NS:(cb + 1) * NS].rearrange("p (b t) -> p b t", b=NB)
                    ins = dve.tensor_copy(smp[:, cb, :, PAD:PAD + NT], src)
                    if cb == 0:
                        E.link(ins)
                E.done(ins, "ctx_out")
                E.need("ctx_out", 3)
                cw, cbias = CP("conv_w"), CP("conv_b")
                for j in range(TAPS):
                    for cb in range(2):
                        src = ctxb[:, cb, j:j + ACCW]
                        if j == 0:
                            ins = dve.tensor_scalar(acc[:, cb, :], src, cw[:, cb * TAPS:cb * TAPS + 1], cbias[:, cb:cb + 1],
                                                    ALU.mult, ALU.add)
                        else:
                            ins = dve.scalar_tensor_tensor(out=acc[:, cb, :], in0=src, scalar=cw[:, cb * TAPS + j:cb * TAPS + j + 1],
                                                           in1=acc[:, cb, :], op0=ALU.mult, op1=ALU.add)
                        E.n += 1
                        ins.then_inc(sem("dve_chain"), 1)
                        if E.n > 1:
                            dve.wait_ge(sem("dve_chain"), E.n - 1)
                dve.wait_ge(sem("dve_chain"), E.n)
                for cb in range(2):
                    for b in range(NB):
                        a = SAMP0 + b * (PAD + NT)
                        ins = dve.tensor_copy(scr[:, cb * NS + b * NT:cb * NS + (b + 1) * NT], acc[:, cb, a:a + NT])
                    E.done(ins, "conv_done")
                E.need("conv_done", 2)
                for t in range(TILES):
                    n = ROWS[t]
                    E.need("conv_tr", t + 1)
                    E.done(dve.tensor_copy(h[0:n, GATE, t, :], ps[t % 2][0:n, 0:256]), "conv_out")
                E.need("conv_out", 5)
                E.done(group_norm(h[:, GATE], 1, 256, stats, RP("conv_ln_g"), RP("conv_ln_b"), h[:, GATE]), "conv_norm")
                E.need("proj_out", (V + 1) * TILES)
                E.done(group_norm(h[:, V], 4, 64, stats, RP("sgu_ln_g"), RP("sgu_ln_b"), h[:, V]), "sgu_vn")
                for g in range(4):
                    if g % 2 == 0:
                        E.need("sgu_z", g // 2 + 1)
                    uu = h[:, U, 0:4, g * 64:(g + 1) * 64]
                    z = ps[6 + g // 2][:, (g % 2) * 256:(g % 2) * 256 + 256].rearrange("p (t c) -> p t c", t=4)
                    dve.scalar_tensor_tensor(out=uu, in0=z, scalar=CP("sgu_b")[:, g:g + 1], in1=uu, op0=ALU.add, op1=ALU.mult)
                E.need("sgu_z", 3)
                for g in range(4):
                    uu = h[0:NS, U, 4, g * 64:(g + 1) * 64]
                    ins = dve.scalar_tensor_tensor(out=uu, in0=ps[5][0:NS, g * 64:(g + 1) * 64],
                                                   scalar=CP("sgu_b_s")[0:NS, g:g + 1], in1=uu, op0=ALU.add, op1=ALU.mult)
                E.done(ins, "sgu_y")
                for k in range(1, 8, 2):
                    E.need("qk_tr", k + 1)
                    E.done(dve.tensor_copy(xT[:, k, 0:SEQ], ps[1][:, :]), "qk_dve")
                E.link(dve.memset(ret_S, 0.0))
                mask = C("ret_mask")
                qd = C("q_decay").rearrange("p (t h) -> p t h", t=TILES)

                def mask_scores(n):
                    E.need("ret_s", n + 1)
                    if n >= 2:
                        E.need("ret_o", n - 1)
                    for hh in range(2):
                        b = ps[((2, 5), (6, 7))[n % 2][hh]]
                        dst = pT[n % 2].rearrange("p (c g k) -> p c g k", c=2, g=2)[:, :, hh, :]
                        m = mask.rearrange("p (c g k) -> p c g k", c=2, g=2)[:, :, hh, :]
                        ins = dve.tensor_tensor(dst, b[:, 0:256].rearrange("p (c k) -> p c k", c=2), m, ALU.mult)
                    E.done(ins, "ret_a")

                mask_scores(0)
                for n in range(4):
                    if n < 3:
                        mask_scores(n + 1)
                    E.need("ret_o", n + 1)
                    for hh in range(2):
                        dst = h[:, RQ, n, :].rearrange("p (c g e) -> p c g e", c=2, g=2)[:, :, hh, :]
                        dec = qd[:, n, :].rearrange("p (c g) -> p c g", c=2)[:, :, hh]
                        dve.tensor_tensor(dst, ps[(3, 1)[hh]][:, 0:128].rearrange("p (c e) -> p c e", c=2),
                                          dec.unsqueeze(2).to_broadcast([128, 2, HD]), ALU.mult)
                    for hp in range(2):
                        for hh in range(2):
                            r = slice(64 * hh, 64 * hh + 64)
                            ins = dve.scalar_tensor_tensor(out=ret_S[r, hp, :], in0=ret_S[r, hp, :], scalar=C("c_decay")[r, hp:hp + 1],
                                                           in1=ps[4][r, hp * 128 + hh * 64:hp * 128 + hh * 64 + 64],
                                                           op0=ALU.mult, op1=ALU.add)
                    E.done(ins, "ret_upd")
                    E.need("ret_upd", n + 1)
                E.need("ret_s", 5)
                for hh in range(2):
                    dst, m = (z[0:NS, 0:NH * NS].rearrange("p (c g k) -> p c g k", c=2, g=2)[:, :, hh, :]
                              for z in (sm[0], C("ret_mask_s")))
                    ins = dve.tensor_tensor(dst, ps[(2, 5)[hh]][0:NS, 0:2 * NS].rearrange("p (c k) -> p c k", c=2), m, ALU.mult)
                E.done(ins, "ret_a")
                E.need("smp_o", 1)
                dve.tensor_tensor(h[0:NS, RQ, 4, :].rearrange("p (h c) -> p h c", h=NH),
                                  ps[3][0:NS, 0:256].rearrange("p (h c) -> p h c", h=NH),
                                  qd[0:NS, 4, :].unsqueeze(2).to_broadcast([NS, NH, HD]), ALU.mult)
                s0 = CP("ret_state").rearrange("p (c n) -> p c n", c=2)
                for hp in range(2):
                    ins = dve.scalar_tensor_tensor(out=s0[:, hp, :], in0=s0[:, hp, :], scalar=C("c_decay_s")[:, hp:hp + 1],
                                                   in1=ps[4 + hp][:, :], op0=ALU.mult, op1=ALU.add)
                E.done(ins, "smp_upd")
                E.need("smp_upd", 1)

                def attend(u):
                    i = u // 4
                    n = (i + 1) * 128
                    E.need("att_s", u + 1)
                    if u >= 2:
                        E.need("att_t", u - 1)
                    b = ps[2] if u % 2 == 0 else ps[5]
                    E.link(dve.scalar_tensor_tensor(out=sm[u % 2][:, 0:n], in0=b[:, 0:n], scalar=SCALE,
                                                    in1=C("attn_bias")[:, (3 - i) * 128:512], op0=ALU.mult, op1=ALU.add))
                    E.link(dve.tensor_reduce(small[:, 8 + u % 2:9 + u % 2], sm[u % 2][:, 0:n], AX, ALU.max))
                    E.done(dve.tensor_scalar(small[:, u % 2:u % 2 + 1], small[:, 8 + u % 2:9 + u % 2], -1.0, None, ALU.mult), "att_m")

                attend(0)
                for u in range(16):
                    i, hd = u // 4, u % 4
                    if u < 15:
                        attend(u + 1)
                    E.need("att_p", u + 1)
                    E.link(dve.reciprocal(small[:, 10 + u % 2:11 + u % 2], small[:, 2 + u % 2:3 + u % 2]))
                    E.need("att_o", u + 1)
                    bo = ps[4] if u % 2 == 0 else ps[7]
                    E.done(dve.tensor_scalar(h[:, SQ, i, hd * HD:(hd + 1) * HD], bo[:, 0:HD], small[:, 10 + u % 2:11 + u % 2],
                                             None, ALU.mult), "att_y")
                E.need("kv_used", NB)
                sbias = C("sample_bias")
                for a, n, b in ((0, 512, 0), (512, 128, 1), (640, NS, 2)):
                    E.link(dve.scalar_tensor_tensor(out=ss[:, a:a + n], in0=ps[b][:, 0:n], scalar=SCALE, in1=sbias[:, a:a + n],
                                                    op0=ALU.mult, op1=ALU.add))
                E.link(dve.tensor_reduce(small[:, 6:7], ss, AX, ALU.max))
                E.done(dve.tensor_scalar(small[:, 4:5], small[:, 6:7], -1.0, None, ALU.mult), "smp_m")
                E.need("smp_p", 1)
                E.link(dve.reciprocal(small[:, 7:8], small[:, 5:6]))
                E.done(dve.tensor_scalar(ss, ss, small[:, 7:8], None, ALU.mult), "smp_n")
                E.need("kv_used", 16)
                o4 = ps[4][:, 0:128].rearrange("p (b c g t) -> p c b g t", b=NB, c=2, g=2)
                for hp in range(2):
                    for hh in range(2):
                        r = slice(64 * hh, 64 * hh + 64)
                        ins = dve.tensor_copy(sm[0][r, hp * NS:(hp + 1) * NS].rearrange("p (b t) -> p b t", b=NB),
                                              o4[r, hp, :, hh, :])
                        if (hp, hh) != (1, 1):
                            E.link(ins)
                E.done(ins, "smp_oT")
                E.need("smp_back", 1)
                E.done(dve.tensor_copy(h[0:NS, SQ, 4, :], ps[5][0:NS, 0:256]), "smp_y")
                E.link(group_norm(h[:, RQ], 4, 64, stats, RP("ret_gn_g"), None, h[:, RQ]))
                E.done(dve.tensor_tensor(h[:, RQ], h[:, RQ], h[:, RG], ALU.mult), "ret_y")
                turn_out()
                for c in range(NOUT):
                    for t in range(TILES):
                        n = ROWS[t]
                        E.need("wout", c * TILES + t + 1)
                        xs = x[0:n, t, c * CW:(c + 1) * CW]
                        E.done(dve.scalar_tensor_tensor(out=xs, in0=xs, scalar=ALPHA, in1=ps[2 + t][0:n, 0:CW],
                                                        op0=ALU.mult, op1=ALU.add), "wout_out")
                E.need("wout_out", 20)

                def row_stats(t, where):
                    n = ROWS[t]
                    for k in range(2):
                        E.link(dve.bn_stats(bn[0:n, t, k, :], x[0:n, t, k * 512:(k + 1) * 512]))
                    E.link(dve.bn_aggr(where[0:n, t, 0:2], bn[0:n, t, :, :]))

                def row_norm(t, where, gain, bias, done):
                    n = ROWS[t]
                    E.link(dve.tensor_scalar(x[0:n, t, :], x[0:n, t, :], where[0:n, t, 0:1], where[0:n, t, 2:3],
                                             ALU.subtract, ALU.mult))
                    E.link(dve.tensor_tensor(x[0:n, t, :], x[0:n, t, :], RP(gain)[0:n, :], ALU.mult))
                    E.done(dve.tensor_tensor(x[0:n, t, :], x[0:n, t, :], RP(bias)[0:n, :], ALU.add), done)

                E.link(dve.memset(mv, 1.0))
                for t in range(TILES):
                    row_stats(t, mv)
                E.done(dve.tensor_scalar(mv[:, :, 3], mv[:, :, 1], EPS, None, ALU.add), "x1_stat")
                E.need("x1_pow", 1)
                for t in range(TILES):
                    row_norm(t, mv, "ln1_g", "ln1_b", "x1")
                turn_out()

                T = TILES

                def r(a, *dims):
                    n = 1
                    for d in dims:
                        n *= d
                    names = "abc"[:len(dims)]
                    ap = R[:, a:a + n]
                    if len(dims) == 2:
                        ap = ap.rearrange("p (a b) -> p a b", a=dims[0])
                    if len(dims) == 3:
                        ap = ap.rearrange("p (a b c) -> p a b c", a=dims[0], b=dims[1])
                    return ap

                memb = r(0, T, NE)
                lg = r(160, T, 36)
                ex = r(400, T, NG)
                exs = R[:, 400:420]
                ex2 = R[:, 440:445]
                gmax, gsum, smax, m1, m2, s1, s2, den = (R[:, 450 + 5 * k:455 + 5 * k] for k in range(8))
                ohg = r(500, T, NG)
                sc4 = r(520, T, NG)
                esel = r(540, T, EPG)
                oh1 = r(580, T, EPG)
                oh2 = r(620, T, EPG)
                sc8 = r(660, T, EPG)
                e1 = r(700, T, NG, EPG)
                e2 = r(860, T, NG, EPG)
                pos = r(1020, T, NE)
                lap = r(1180, T, NE)
                item = r(1340, T, NE)
                tmp = r(1500, T, NE)
                over = R[:, 1660:1692]
                cs = [R[:, 1692:1740], R[:, 1740:1788]]
                w12 = r(1790, 2, T)
                p12 = r(1800, 2, T)
                sl = r(1810, 2, T)
                eid = R[:, 1820:1820 + NI - NE]
                tot = R[:, 1850:1851]
                hv = R[:, 1852:1852 + 24]

                def bc(ap, dims):
                    return ap.to_broadcast(dims)

                E.need("logits", 1)
                E.link(dve.memset(R[:, 160:340], 0.0))
                E.link(dve.tensor_copy(lg[:, 0:4, :], ps[2][:, 0:144].rearrange("p (t n) -> p t n", t=4)))
                E.link(dve.tensor_copy(lg[0:NS, 4, :], ps[2][0:NS, 144:180]))
                bias = rowpar[:, row_at["router_g_b"][0]:row_at["router_g_b"][0] + 36]
                E.link(dve.tensor_tensor(lg, lg, bc(bias.unsqueeze(1), [128, T, 36]), ALU.add))
                g = lg[:, :, 0:NG]
                E.link(dve.tensor_reduce(gmax, g, AX, ALU.max))
                E.done(dve.tensor_tensor(ex, g, bc(gmax.unsqueeze(2), [128, T, NG]), ALU.subtract), "ex_in")

                def first_max(onehot, values, top, table, score, n):
                    E.link(dve.tensor_tensor(score, values, bc(top.unsqueeze(2), [128, T, n]), ALU.is_equal))
                    E.link(dve.tensor_tensor(score, score, bc(table.unsqueeze(1), [128, T, n]), ALU.mult))
                    E.link(dve.tensor_reduce(smax, score, AX, ALU.max))
                    E.link(dve.tensor_tensor(onehot, score, bc(smax.unsqueeze(2), [128, T, n]), ALU.is_equal))

                first_max(ohg, g, gmax, C("first4"), sc4, NG)
                ev = lg[:, :, NG:36].rearrange("p t (g e) -> p t g e", g=NG)
                E.link(dve.tensor_tensor(e1, ev, bc(ohg.unsqueeze(3), [128, T, NG, EPG]), ALU.mult))
                E.link(dve.tensor_reduce(esel, e1.rearrange("p t g e -> p t e g"), AX, ALU.add))
                E.link(dve.tensor_reduce(m1, esel, AX, ALU.max))
                first_max(oh1, esel, m1, C("first8"), sc8, EPG)
                E.link(dve.scalar_tensor_tensor(out=esel, in0=oh1, scalar=NEG, in1=esel, op0=ALU.mult, op1=ALU.add))
                E.link(dve.tensor_reduce(m2, esel, AX, ALU.max))
                E.done(dve.tensor_tensor(ex2, m2, m1, ALU.subtract), "ex2_in")
                first_max(oh2, esel, m2, C("first8"), sc8, EPG)
                E.need("ex_out", 1)
                E.link(dve.tensor_reduce(gsum, ex, AX, ALU.add))
                E.need("ex2_out", 1)
                E.link(dve.tensor_scalar(den, ex2, 1.0, None, ALU.add))
                E.link(dve.tensor_tensor(den, den, gsum, ALU.mult))
                E.link(dve.reciprocal(gates[:, 0, :], den))
                E.link(dve.tensor_tensor(gates[:, 1, :], gates[:, 0, :], ex2, ALU.mult))
                valid = C("valid")
                for e, oh in ((e1, oh1), (e2, oh2)):
                    E.link(dve.tensor_tensor(e, bc(ohg.unsqueeze(3), [128, T, NG, EPG]), bc(oh.unsqueeze(2), [128, T, NG, EPG]),
                                             ALU.mult))
                    e3 = e.rearrange("p t g e -> p t (g e)")
                    E.link(dve.tensor_tensor(e3, e3, bc(valid.unsqueeze(2), [128, T, NE]), ALU.mult))
                e1f, e2f = (e.rearrange("p t g e -> p t (g e)") for e in (e1, e2))
                E.done(dve.tensor_tensor(memb, e1f, e2f, ALU.add), "member")
                E.need("counts", 1)
                E.link(dve.tensor_scalar(over, ps[4][:, 0:NE], float(BLK), None, ALU.is_gt))
                for k in range(2, (MAXCNT + BLK - 1) // BLK):
                    E.link(dve.scalar_tensor_tensor(out=over, in0=ps[4][:, 0:NE], scalar=float(k * BLK), in1=over,
                                                    op0=ALU.is_gt, op1=ALU.add))
                E.link(dve.memset(cs[0], 0.0))
                E.link(dve.memset(cs[1], 0.0))
                E.link(dve.tensor_copy(cs[0][:, 16:48], over))
                for k, d in enumerate((1, 2, 4, 8, 16)):
                    a, b = cs[k % 2], cs[(k + 1) % 2]
                    E.link(dve.tensor_tensor(b[:, 16:48], a[:, 16:48], a[:, 16 - d:48 - d], ALU.add))
                incl = cs[1][:, 16:48]
                E.link(dve.tensor_copy(pos.rearrange("p t e -> p (t e)"), ps[3][:, 0:T * NE]))
                E.link(dve.tensor_scalar(lap, pos, float(BLK), None, ALU.is_ge))
                for k in range(2, (MAXCNT + BLK - 1) // BLK):
                    E.link(dve.scalar_tensor_tensor(out=lap, in0=pos, scalar=float(k * BLK), in1=lap, op0=ALU.is_ge, op1=ALU.add))
                E.link(dve.scalar_tensor_tensor(out=pos, in0=lap, scalar=-float(BLK), in1=pos, op0=ALU.mult, op1=ALU.add))
                eio = C("iota")[:, 0:NE]
                E.link(dve.tensor_tensor(over, incl, over, ALU.subtract))
                E.link(dve.tensor_scalar(over, over, float(NE - 1), None, ALU.add))
                E.link(dve.tensor_tensor(over, over, eio, ALU.subtract))
                E.link(dve.tensor_tensor(item, lap, bc(over.unsqueeze(1), [128, T, NE]), ALU.add))
                E.link(dve.tensor_scalar(tmp, lap, 0.5, None, ALU.is_ge))
                E.link(dve.tensor_tensor(item, item, tmp, ALU.mult))
                E.link(dve.tensor_tensor(item, item, bc(eio.unsqueeze(1), [128, T, NE]), ALU.add))
                for k, e in enumerate((e1f, e2f)):
                    E.link(dve.tensor_tensor(tmp, e, item, ALU.mult))
                    E.link(dve.tensor_reduce(w12[:, k, :], tmp, AX, ALU.add))
                    E.link(dve.tensor_tensor(tmp, e, pos, ALU.mult))
                    E.link(dve.tensor_reduce(p12[:, k, :], tmp, AX, ALU.add))
                E.link(dve.scalar_tensor_tensor(out=sl, in0=w12, scalar=float(BLK), in1=p12, op0=ALU.mult, op1=ALU.add))
                E.link(dve.tensor_copy(slots[:], sl))
                place, whose = onehots(R)
                iota = C("iota")
                for k in range(2):
                    pk = place[:, k * T:(k + 1) * T, :]
                    wk = whose[:, k * T:(k + 1) * T, :]
                    E.link(dve.tensor_tensor(pk, bc(iota.unsqueeze(1), [128, T, 128]), bc(p12[:, k, :].unsqueeze(2), [128, T, 128]),
                                             ALU.is_equal))
                    E.link(dve.tensor_tensor(wk, bc(iota[:, 0:NI].unsqueeze(1), [128, T, NI]),
                                             bc(w12[:, k, :].unsqueeze(2), [128, T, NI]), ALU.is_equal))
                    ins = dve.tensor_tensor(wk, wk, bc(C("tok").unsqueeze(2), [128, T, NI]), ALU.mult)
                    if k == 0:
                        E.link(ins)
                E.done(ins, "onehot")
                nov = NI - NE
                big = R[:, 1020:1020 + nov * NE].rearrange("p (o e) -> p o e", o=nov)
                E.link(dve.tensor_tensor(big, bc(incl.unsqueeze(1), [128, nov, NE]), bc(iota[:, 0:nov].unsqueeze(2), [128, nov, NE]),
                                         ALU.is_le))
                E.link(dve.tensor_reduce(eid, big, AX, ALU.add))
                E.link(dve.tensor_scalar(eid, eid, float(NE - 1), None, ALU.min))
                E.link(dve.tensor_copy(items[0:1, 0:NE], iota[0:1, 0:NE]))
                E.link(dve.tensor_copy(items[0:1, NE:NI], eid[0:1, :]))
                E.link(dve.tensor_scalar(hv[:, 0:nov // 2], iota[:, 0:nov // 2], 2.0, None, ALU.mult))
                E.link(dve.tensor_scalar(hv[:, 0:nov // 2], hv[:, 0:nov // 2], incl[:, NE - 1:NE], None, ALU.is_lt))
                E.link(dve.tensor_reduce(tot, hv[:, 0:nov // 2], AX, ALU.add))
                E.link(dve.tensor_copy(trip[0:1, 0:1], cum[0:1, 0:1]))
                E.link(dve.tensor_scalar(tot, tot, float(NE // 2), None, ALU.add))
                E.link(dve.tensor_tensor(cum[0:1, 0:1], cum[0:1, 0:1], tot[0:1, :], ALU.add))
                E.link(dve.tensor_copy(trip[0:1, 1:2], tot[0:1, :]))
                E.need("idx_ps", 1)
                E.done(dve.tensor_copy(sidx[:], ps[5][:, 0:NI]), "routed")
                E.need("routed", 1)

                lo = dve.value_load(trip[0:1, 0:1], min_val=1, max_val=1 + (DEPTH - 1) * NI // 2)
                turns = dve.value_load(trip[0:1, 1:2], min_val=NE // 2, max_val=NI // 2)
                with dve.Fori(0, turns) as turn:
                    i = dve.snap(lo + turn)
                    for q in range(2):
                        dve.wait_ge(sem(f"xg_tr1_{q}"), i + 1)
                        dve.tensor_copy(xgT[q][:, 4:8, :], ps[1][:, 0:4 * BLK].rearrange("p (c m) -> p c m", c=4))\
                           .then_inc(sem(f"xgT_dve{q}"), 1)
                    for q in range(2):
                        dve.wait_ge(sem(f"sg{q}"), i + 1)
                        dve.wait_ge(sem(f"w1_used{q}"), i + 1)
                        dve.tensor_tensor(hm[q], ps[3 + 2 * q][0:BLK, :], sg[q], ALU.mult).then_inc(sem(f"hm{q}"), 1)
                    for q in range(2):
                        dve.wait_ge(sem(f"y1_ps{q}"), i + 1)
                        dve.wait_ge(sem(f"y_stored{q}"), i * 16)
                        dve.tensor_copy(yo[q][:, 512:1024], ps[7][0:BLK, :]).then_inc(sem(f"y_dve{q}"), 1)
                for t in range(TILES):
                    n = ROWS[t]
                    q = t % 2
                    dve.wait_ge(sem(f"y_got{q}"), (L * (3 - q) + t // 2 + 1) * 32)
                    E.link(dve.tensor_scalar(x[0:n, t, :], x[0:n, t, :], ALPHA, None, ALU.mult))
                    for k in range(2):
                        E.link(dve.scalar_tensor_tensor(out=x[0:n, t, :], in0=ygot[q][k][0:n, :], scalar=gates[0:n, k, t:t + 1],
                                                        in1=x[0:n, t, :], op0=ALU.mult, op1=ALU.add))
                    row_stats(t, mv)
                    E.done(dve.tensor_scalar(mv[0:n, t, 3:4], mv[0:n, t, 1:2], EPS, None, ALU.add), "x2_stat")
                    E.need("x2_pow", t + 1)
                    row_norm(t, mv, "ln2_g", "ln2_b", "x2")

        @block.gpsimd
        def _(pool):
            E = Eng(pool, "pool")
            pool.memset(h[:, :, 4, :], 0.0).then_inc(sem("pinit"), 1)
            pool.memset(halfc[:], -0.5).then_inc(sem("pinit"), 1)
            pool.memset(pscr, 0.0).then_inc(sem("pinit"), 1)
            pool.wait_ge(sem("pinit"), 3)
            for q in range(2):
                for name in ("w0_used", "w1_used", "xg_tr0_", "xg_tr1_", "xgT_act", "xgT_dve", "sg", "hm", "hm_tr", "hT",
                             "y0_ps", "y1_ps", "y_act", "y_dve", "gidx"):
                    pool.sem_inc(sem(f"{name}{q}"), 1)
                for name in ("w0_", "w1_", "w2_", "y_stored"):
                    pool.sem_inc(sem(f"{name}{q}"), 16)
            for k in range(NI - NE):
                pool.dma_start(yd[(NE + k) * BLK:(NE + k + 1) * BLK, :], pscr[0:BLK, 0:D]).then_inc(sem("yd_clear"), 16)
            pool.wait_ge(sem("yd_clear"), 16 * (NI - NE))
            pool.wait_ge(start_sem, 16 * (1 + TILES))
            for L in range(DEPTH):
                E.L = L
                st_n = [0]

                def inv_root(n):
                    st_n[0] += 1
                    E.need("st_in", st_n[0])
                    var = pstat[:, n:2 * n]
                    E.done(pool.tensor_tensor(var, var, halfc[:, 0:n], ALU.pow), "st_out")

                E.need("par_in", 32)
                E.link(pool.memset(ctxb[:, :, 0:PAD], 0.0))
                smp = ctxb[:, :, SAMP0:CTXW].rearrange("p c (b w) -> p c b w", b=NB)
                st = CP("conv_state").rearrange("p (c b w) -> p c b w", c=2, b=NB)
                for cb in range(2):
                    E.link(pool.tensor_copy(smp[:, cb, :, 0:PAD], st[:, cb]))
                E.link(pool.memset(smp[:, :, :, PAD:PAD + NT], 0.0))
                E.done(pool.memset(QB, 0.0), "ctx_pool")
                E.need("proj_out", (GATE + 1) * TILES)
                E.done(pool.tensor_tensor(h[:, VAL], h[:, VAL], h[:, GATE], ALU.mult), "glu")
                wT = CP("sgu_wT").rearrange("p (g t) -> p g t", g=4)
                wTs = CP("sgu_wT_s").rearrange("p (g t) -> p g t", g=4)
                E.link(pool.tensor_tensor(wT, wT, C("sgu_mask").unsqueeze(1).to_broadcast([128, 4, 128]), ALU.mult))
                E.done(pool.tensor_tensor(wTs[0:NS], wTs[0:NS], C("sgu_mask_s")[0:NS].unsqueeze(1).to_broadcast([NS, 4, NS]),
                                          ALU.mult), "sgu_w")

                def rotate(s, half_dim, cos, sin):
                    rows = h[:, s].rearrange("p t (h c) -> p t h c", h=NH)
                    n = half_dim
                    a, b = rows[:, :, :, 0:n], rows[:, :, :, n:2 * n]
                    m = TILES * NH * n
                    t1 = pscr[:, 0:m].rearrange("p (t h c) -> p t h c", t=TILES, h=NH)
                    t2 = pscr[:, m:2 * m].rearrange("p (t h c) -> p t h c", t=TILES, h=NH)
                    co = C(cos).rearrange("p (t c) -> p t c", t=TILES)
                    si = C(sin).rearrange("p (t c) -> p t c", t=TILES)
                    for t in range(TILES):
                        cb = co[:, t, :].unsqueeze(1).to_broadcast([128, NH, n])
                        sb_ = si[:, t, :].unsqueeze(1).to_broadcast([128, NH, n])
                        pool.tensor_tensor(t1[:, t], a[:, t], sb_, ALU.mult)
                        pool.tensor_tensor(t2[:, t], b[:, t], sb_, ALU.mult)
                        pool.tensor_tensor(a[:, t], a[:, t], cb, ALU.mult)
                        ins = pool.tensor_tensor(b[:, t], b[:, t], cb, ALU.mult)
                    E.link(ins)
                    E.link(pool.tensor_tensor(a, a, t2, ALU.subtract))
                    ins = pool.tensor_tensor(b, b, t1, ALU.add)
                    return ins

                E.need("proj_out", (RK + 1) * TILES)
                E.link(rotate(RQ, 32, "rcos", "rsin"))
                E.done(rotate(RK, 32, "kcos", "ksin"), "rot_r")
                E.need("proj_out", (SK + 1) * TILES)
                E.need("rot_r", 1)
                E.link(rotate(SQ, 8, "scos", "ssin"))
                E.done(rotate(SK, 8, "scos", "ssin"), "rot_s")
                inv_root(TILES)
                inv_root(4 * TILES)
                E.need("qk_tr", 9)
                kd = C("k_decay").rearrange("p (t h) -> p t h", t=TILES)
                for t in range(TILES):
                    kr = h[:, RK, t, :].rearrange("p (h c) -> p h c", h=NH)
                    ins = pool.tensor_tensor(kr, kr, kd[:, t, :].unsqueeze(2).to_broadcast([128, NH, HD]), ALU.mult)
                E.done(ins, "k_dec")
                E.need("k_dec", 1)
                E.need("conv_tr", 5)
                own = C("own")[0:NS, :]
                for hd in range(NH):
                    vv = h[0:NS, RV, 4, hd * HD:(hd + 1) * HD].unsqueeze(1).to_broadcast([NS, NB, HD])
                    ins = pool.tensor_tensor(vexp[:, hd], vv, own.unsqueeze(2).to_broadcast([NS, NB, HD]), ALU.mult)
                E.done(ins, "vexp")
                E.need("vexp", 1)
                E.need("qk_act", 5)
                for hp in range(2):
                    qb = QB[:, hp, :].rearrange("p (c w) -> p c w", c=4)
                    src = xT[:, 4 + hp, SEQ:NTOK].rearrange("p (c b t) -> p c b t", c=4, b=2)
                    for bb in range(2):
                        for hh in range(2):
                            r = slice(64 * hh, 64 * hh + 64)
                            at = 48 * bb + 4 * (2 * hp + hh)
                            ins = pool.tensor_copy(qb[r, :, at:at + NT], src[r, :, bb, :])
                            if (hp, bb, hh) != (1, 1, 1):
                                E.link(ins)
                E.done(ins, "qb_ok")
                E.need("qb_ok", 1)
                inv_root(4 * TILES)
                E.need("x1_stat", 1)
                E.done(pool.tensor_tensor(mv[:, :, 2], mv[:, :, 3], halfc[:, 0:TILES], ALU.pow), "x1_pow")
                E.need("routed", 1)
                E.need("x1_store", 16 * TILES)
                lo = pool.value_load(trip[0:1, 0:1], min_val=1, max_val=1 + (DEPTH - 1) * NI // 2)
                turns = pool.value_load(trip[0:1, 1:2], min_val=NE // 2, max_val=NI // 2)
                with pool.Fori(0, turns) as turn:
                    i = pool.snap(lo + turn)
                    for q in range(2):
                        col = pool.snap(turn * 2 + q)
                        pool.wait_ge(sem(f"xg_tr1_{q}"), i)
                        pool.sem_inc(sem(f"gidx{q}"), -1)
                        pool.tensor_copy(gidx[q], sidx[:, bass.ds(col, 1)]).then_inc(sem(f"gidx{q}"), 1)
                        pool.wait_ge(sem(f"gidx{q}"), 1)
                        pool.indirect_dma_start(out=xg[q], out_offset=None, in_=x1d,
                                                in_offset=bass.IndirectOffsetOnAxis(ap=gidx[q], axis=0))\
                            .then_inc(sem(f"xg{q}"), 16)
                for q in range(2):
                    pool.wait_ge(sem(f"y_stored{q}"), (lo + turns) * 16)
                def fetch(t):
                    n = ROWS[t]
                    for k in range(2):
                        pool.indirect_dma_start(out=ygot[t % 2][k][0:n, :], out_offset=None, in_=yd,
                                                in_offset=bass.IndirectOffsetOnAxis(ap=slots[0:n, k, t:t + 1], axis=0))\
                            .then_inc(sem(f"y_got{t % 2}"), 16)

                E.link(pool.tensor_tensor(halfc[:, 1:2], halfc[:, 0:1], halfc[:, 2:3], ALU.pow))
                E.link(pool.memset(halfc[:, 1:2], -0.5))
                fetch(0)
                fetch(1)
                for t in range(TILES):
                    n = ROWS[t]
                    E.need("x2_stat", t + 1)
                    E.done(pool.tensor_tensor(mv[0:n, t, 2:3], mv[0:n, t, 3:4], halfc[0:n, 0:1], ALU.pow), "x2_pow")
                    if t + 2 < TILES:
                        fetch(t + 2)
    wrong = {name: (made.get(name, 0), n) for name, n in PER.items() if made.get(name, 0) != n * DEPTH}
    assert not wrong, wrong


def layout(a):
    c = np.ascontiguousarray
    w_in, L = a["w_in"], DEPTH
    order = [7, 8, 9, 10, 3, 0, 1, 2, 4, 5, 6]
    blocks = w_in.reshape(L, KT, 128, NCH, CW)[:, :, :, order]
    proj = blocks.transpose(0, 3, 2, 1, 4)
    outp = a["w_out"].reshape(L, KT, 128, NOUT, CW).transpose(0, 3, 2, 1, 4)
    w_proj = c(np.concatenate([proj, outp], 1)).reshape(L * (NCH + NOUT), 128, KT * CW)

    def keys(cache):
        cache = cache.reshape(L, NB, PAST, 256)
        far = cache[:, :, :512].reshape(L, NB, 32, 16, 256)[:, :, :, :4].reshape(L, NB, 128, 256)
        return np.concatenate([cache[:, :, 512:], far], 2)

    k = keys(a["cache_swa_k"]).transpose(0, 1, 3, 2).reshape(L, NB, 2, 128, NKEY).transpose(0, 1, 3, 2, 4)
    v = keys(a["cache_swa_v"]).reshape(L, NB, 5, 128, 256).transpose(0, 1, 3, 2, 4)
    kv = c(np.concatenate([k.reshape(L, NB, 128, 2 * NKEY), v.reshape(L, NB, 128, 2 * NKEY)], 1))
    row = np.concatenate([a[n].reshape(L, -1) for n, _ in ROWPAR], 1)
    rowpar = c(np.broadcast_to(row[:, None], (L, 128, row.shape[1]))).reshape(L * 128, -1)
    sw = a["sgu_w"].transpose(0, 3, 1, 2)

    def rows128(z):
        full = np.zeros((L, 128) + z.shape[2:], np.float32)
        full[:, :z.shape[1]] = z
        return full

    col = dict(
        conv_w=a["conv_w"].reshape(L, TAPS, 2, 128).transpose(0, 3, 2, 1),
        conv_b=a["conv_b"].reshape(L, 2, 128).transpose(0, 2, 1),
        sgu_wT=sw,
        sgu_wT_s=rows128(np.tile(sw[:, :NT, :, :NT], (1, NB, 1, NB))),
        sgu_b=a["sgu_b"].transpose(0, 2, 1),
        sgu_b_s=rows128(np.tile(a["sgu_b"][:, :, :NT].transpose(0, 2, 1), (1, NB, 1))),
        router_w=np.concatenate([a["router_g_w"], a["router_e_w"].transpose(0, 2, 1, 3).reshape(L, D, NE)], 2)
        .reshape(L, KT, 128, NG + NE).transpose(0, 2, 1, 3),
        conv_state=a["state_conv"].reshape(L, NB, PAD, 2, 128).transpose(0, 4, 3, 1, 2),
        ret_state=a["state_ret"].reshape(L, NB, 2, 2, HD, HD).transpose(0, 3, 4, 2, 1, 5),
    )
    colpar = c(np.concatenate([col[n].reshape(L, 128, -1) for n, _ in COLPAR], 2)).reshape(L * 128, -1)
    return dict(
        x_in=c(np.concatenate([a["x_prompt"].reshape(SEQ, D), a["x_sample"].reshape(NS, D)], 0)),
        w_proj=w_proj, kv=kv.reshape(L * 16, 128, 2 * NKEY), rowpar=rowpar, colpar=colpar,
        w1=a["moe_w1"].reshape(L * NE, 128, KT * FF), w3=a["moe_w3"].reshape(L * NE, 128, KT * FF),
        w2=a["moe_w2"].reshape(L * NE, 128, 4 * D),
    )


OUTS = dict(y=(NTOK, D), p_ret=(DEPTH, 128, 128), s_ret=(DEPTH, 128, 2 * NB * HD), p_k=(DEPTH, SEQ, 256),
            p_v=(DEPTH, SEQ, 256), s_k=(DEPTH, NS, 256), s_v=(DEPTH, NS, 256), p_conv=(DEPTH, PAD, 256),
            s_conv=(DEPTH, NS, 256), s_sgu=(DEPTH, NS, 256))

def kernel(**inputs):
    import concourse.bacc as bacc
    from concourse.bass_utils import run_bass_kernel_spmd

    arrays = layout({k: np.asarray(v) for k, v in inputs.items()})
    arrays["const"] = shape_constants()[0]
    nc = bacc.Bacc("TRN2", target_bir_lowering=False, num_devices=1)
    io = {n: nc.dram_tensor("in_" + n, v.shape, F32, kind="ExternalInput").ap() for n, v in arrays.items()}
    io |= {n: nc.dram_tensor("out_" + n, s, F32, kind="ExternalOutput").ap() for n, s in OUTS.items()}
    io["x1d"] = nc.dram_tensor("x1d", (NTOK, D), F32, kind="Internal").ap()
    io["yd"] = nc.dram_tensor("yd", (NI * BLK, D), F32, kind="Internal").ap()
    trunk_program(nc, io, shape_constants()[1])
    r = run_bass_kernel_spmd(nc, [{"in_" + n: v for n, v in arrays.items()}], core_ids=[0]).results[0]
    o = {n: r["out_" + n] for n in OUTS}
    L = DEPTH
    p_ret = o["p_ret"].reshape(L, 2, HD, 2, HD).transpose(0, 3, 1, 2, 4).reshape(L, 1, NH, HD, HD)
    s_ret = o["s_ret"].reshape(L, 2, HD, 2, NB, HD).transpose(0, 4, 3, 1, 2, 5).reshape(L, NB, NH, HD, HD)
    return (o["y"][:SEQ].reshape(1, SEQ, D), o["y"][SEQ:].reshape(NB, NT, D), p_ret,
            o["p_k"].reshape(L, 1, SEQ, NH, HD), o["p_v"].reshape(L, 1, SEQ, NH, HD), o["p_conv"].reshape(L, 1, PAD, 256),
            s_ret, o["s_k"].reshape(L, NB, NT, NH, HD), o["s_v"].reshape(L, NB, NT, NH, HD),
            o["s_conv"].reshape(L, NB, NT, 256), o["s_sgu"].reshape(L, NB, NT, 256))
```

```python
from contextlib import ExitStack

import numpy as np
import concourse.bass as bass
from concourse import mybir

F32 = mybir.dt.float32
I32 = mybir.dt.int32
ALU = mybir.AluOpType
ACT = mybir.ActivationFunctionType
AX = mybir.AxisListType.X

D = 1024
SEQ = 512
DEPTH = 2
NB = 8
NT = 4
NS = NB * NT
PAST = 1024
HD = 64
NH = 4
NTOK = SEQ + NS
TILES = 5
ROWS = [128, 128, 128, 128, NS]
KT = D // 128
CW = 256
QW = CW // 4
NCH = 11
NOUT = 4
TAPS = 31
PAD = TAPS - 1
CTXW = PAD + SEQ + NB * (PAD + NT)
ACCW = CTXW - PAD
SAMP0 = PAD + SEQ
NG, EPG, NE = 4, 8, 32
FF = 512
BLK = 128
MAXCNT = NTOK
NOVER = (2 * NTOK) // BLK
NI = (NE + NOVER + 1) // 2 * 2
ALPHA = float((2 * DEPTH) ** 0.25)
EPS = 1e-5
NEG = -1e30
SCALE = HD ** -0.5
NKEY = 640
DIL = ((128, 1), (512, 4), (2048, 16))
CACHES = (0, 2, 1, 3, 4, 6, 5, 7)
VAL, GATE, U, V, RG, RQ, RK, RV, SQ, SK, SV = range(NCH)


def multiplicity(dist):
    m = np.zeros(dist.shape)
    for window, dil in DIL:
        m += (dist >= 0) & (dist <= window) & (dist % dil == 0)
    return np.where(m > 0, np.log(np.maximum(m, 1)), NEG)


def shape_constants():
    p = np.arange(128)
    row_b, row_t = p // NT, p % NT
    g = 1.0 - 2.0 ** (-5.0 - np.arange(NH))
    parts = []

    def put(name, a):
        a = np.asarray(a, np.float64).reshape(a.shape[0], -1)
        full = np.zeros((128, a.shape[1]))
        full[: a.shape[0]] = a
        parts.append((name, full))

    put("ident", np.eye(128))
    put("attn_bias", multiplicity(384 + p[:, None] - np.arange(512)[None]))
    k = np.arange(NKEY - 512)
    idx = np.concatenate([np.arange(512, 1024), 16 * (k // 4) + k % 4, PAST + np.tile(np.arange(NT), NB)])
    owner = np.concatenate([np.full(NKEY, -1), np.repeat(np.arange(NB), NT)])
    rb, rt = p // 16, p % 4
    bias = multiplicity(PAST + rt[:, None] - idx[None])
    put("sample_bias", np.where((owner[None] >= 0) & (owner[None] != rb[:, None]), NEG, bias))
    causal = (p[None, :] >= p[:, None]).astype(float)
    put("ret_mask", causal[:, None, :] * (g[None, :] ** -(p[:, None] + 1.0))[:, :, None])
    s = np.arange(NS)
    same = (s[:, None] // NT == s[None] // NT) & (s[None] % NT >= s[:, None] % NT)
    put("ret_mask_s", same[:, None, :] * (g[None, :] ** -(s[:, None] % NT + 1.0))[:, :, None])
    step = np.stack([p] * 4 + [row_t], 1)
    length = np.array([128] * 4 + [NT])
    put("q_decay", g[None, None] ** (step[:, :, None] + 1.0))
    put("k_decay", g[None, None] ** np.maximum(length[None, :, None] - 1.0 - step[:, :, None], 0))
    head = 2 * np.arange(2)[None] + (p // 64)[:, None]
    put("c_decay", g[head] ** 128.0)
    put("c_decay_s", g[head] ** float(NT))
    pos = np.stack([128 * t + p for t in range(4)] + [np.where(p < NS, PAST + row_t, 0)], 1).astype(np.float32)
    for name, theta, rot in (("r", 10000.0, HD), ("s", 500000.0, HD // 4)):
        inv = np.float32(theta) ** (-np.arange(rot // 2, dtype=np.float32) * np.float32(2.0 / rot))
        ang = (pos[:, :, None] * inv[None, None]).astype(np.float32).astype(np.float64)
        put(name + "cos", np.cos(ang))
        put(name + "sin", np.sin(ang))
        if name == "r":
            put("kcos", np.cos(ang) * SCALE)
            put("ksin", np.sin(ang) * SCALE)
    put("pick", np.eye(128).reshape(128, NB, NH, NT).transpose(0, 2, 1, 3))
    put("parity", np.stack([1 - p // 16 % 2, p // 16 % 2], 1))
    put("sgu_mask", causal)
    put("sgu_mask_s", same.astype(float))
    put("own", (s[:, None] // NT == np.arange(NB)[None]).astype(float))
    put("before", (p[:, None] < p[None, :]).astype(float))
    put("ones", np.ones((128, 128)))
    put("iota", np.tile(np.arange(128), (128, 1)))
    put("first4", np.tile(4.0 - np.arange(4), (128, 1)))
    put("first8", np.tile(8.0 - np.arange(8), (128, 1)))
    tok = 128 * np.arange(TILES)[None] + p[:, None]
    put("tok", np.where(tok < NTOK, tok, 0))
    put("valid", (tok < NTOK).astype(float))
    at, where = {}, 0
    for name, a in parts:
        at[name] = (where, a.shape[1])
        where += a.shape[1]
    return np.concatenate([a for _, a in parts], 1).astype(np.float32), at


ROWPAR = [("ret_gn_g", 256), ("conv_ln_g", 256), ("conv_ln_b", 256), ("sgu_ln_g", 256), ("sgu_ln_b", 256),
          ("ln1_g", D), ("ln1_b", D), ("ln2_g", D), ("ln2_b", D), ("router_g_b", NG), ("router_e_b", NE)]
COLPAR = [("conv_w", 2 * TAPS), ("conv_b", 2), ("sgu_wT", 4 * 128), ("sgu_wT_s", 4 * NS), ("sgu_b", 4),
          ("sgu_b_s", 4), ("router_w", KT * (NG + NE)), ("conv_state", 2 * NB * PAD), ("ret_state", 2 * NB * HD)]


def offsets(fields):
    at, where = {}, 0
    for name, n in fields:
        at[name] = (where, n)
        where += n
    return at, where


PER = dict(par_in=32, xT_tr=30, xT_low=15, xT_high=15, proj=55, proj_out=55,
           glu=1, ctx_tr=3, ctx_out=3, ctx_pool=1, conv_done=2, conv_tr=5, conv_out=5, conv_norm=1, conv_y=1,
           sgu_w=1, sgu_vn=1, sgu_z=3, sgu_y=1, rot_r=1, rot_s=1, qk_tr=9, qk_act=5, qk_dve=4, k_dec=1,
           ret_s=5, ret_a=5, ret_o=4, ret_kv=4, ret_upd=4, smp_o1=1, smp_o1c=1, vexp=1, smp_o=1, smp_upd=1, ret_y=1, ret_mean=1, ret_sq=1,
           att_s=16, att_m=16, att_p=16, att_t=16, att_pT=16, att_o=16, att_y=16,
           qb_ok=1, kv_used=16, smp_m=1, smp_p=1, smp_n=1, smp_t=1, smp_pT=1, smp_rows=1,
           smp_back=1, smp_y=1, stores=16 * 9, wout=20, wout_out=20, x1=5, x1_store=80, x1_stat=5, x1_pow=5,
           logits=1, ex_in=1, ex_out=1, ex2_in=1, ex2_out=1, member=1, counts=1, places=1, onehot=1, idx_ps=1,
           routed=1, x2_stat=5, x2_pow=5, x2=5,
           st_in=3, st_out=3)


def trunk_program(nc, io, const_at):
    made = {}
    row_at, row_n = offsets(ROWPAR)
    col_at, col_n = offsets(COLPAR)
    ctx = ExitStack()
    with ctx:
        def sb(name, shape, dt=F32):
            return ctx.enter_context(nc.sbuf_tensor(name, shape, dt))[:]

        sems = {}

        def sem(name):
            if name not in sems:
                sems[name] = ctx.enter_context(nc.semaphore(name))
            return sems[name]

        x = sb("x", [128, TILES, D])
        xT = sb("xT", [128, KT, NTOK])
        const = sb("const", [128, sum(n for _, n in const_at.values())])
        rowpar = sb("rowpar", [128, row_n])
        colpar = sb("colpar", [128, col_n])
        small = sb("small", [128, 64])
        trip = sb("trip", [1, 2], I32)
        cum = sb("cum", [1, 2])
        items = sb("items", [1, NI], I32)
        slots = sb("slots", [128, 2, TILES], I32)
        gates = sb("gates", [128, 2, TILES])
        sidx = sb("sidx", [128, NI], I32)
        pstat = sb("pstat", [128, 2 * 4 * TILES])
        mv = sb("mv", [128, TILES, 4])
        bn = sb("bn", [128, TILES, 2, 6])
        halfc = sb("halfc", [128, 4 * TILES])

        def C(name):
            a, n = const_at[name]
            return const[:, a:a + n]

        def RP(name):
            a, n = row_at[name]
            return rowpar[:, a:a + n]

        def CP(name):
            a, n = col_at[name]
            return colpar[:, a:a + n]

        HCOLS = NCH * TILES * CW
        WCOLS = 4096
        ARENA = 32048
        arena = sb("arena", [128, ARENA])
        cursor = [0]

        def carve(n):
            a = cursor[0]
            cursor[0] += n
            assert cursor[0] <= ARENA, (cursor[0], ARENA)
            return arena[:, a:a + n]

        h = carve(HCOLS).rearrange("p (s t c) -> p s t c", s=NCH, t=TILES)
        ring = [carve(KT * CW).rearrange("p (k c) -> p k c", k=KT) for _ in range(2)]
        NKV = 4
        kv = [carve(2 * NKEY) for _ in range(NKV - 1)]
        VEXP = NH * NB * HD
        ctx_acc = carve(max(2 * CTXW + 2 * ACCW, VEXP + 2 * NKEY))
        kv.append(ctx_acc[:, VEXP:VEXP + 2 * NKEY])
        ctxb = ctx_acc[:, 0:2 * CTXW].rearrange("p (c w) -> p c w", c=2)
        acc = ctx_acc[:, 2 * CTXW:2 * CTXW + 2 * ACCW].rearrange("p (c w) -> p c w", c=2)
        vexp = ctx_acc[0:NS, 0:NH * NB * HD].rearrange("p (h b e) -> p h b e", h=NH, b=NB)
        ret_S = carve(2 * HD).rearrange("p (c e) -> p c e", c=2)
        sm = [carve(512) for _ in range(2)]
        pT = [carve(512) for _ in range(2)]
        ss = carve(672)
        PTs = carve(6 * 128).rearrange("p (k r) -> p k r", k=6)
        QB = carve(2 * NB * 32).rearrange("p (c q) -> p c q", c=2)
        scr = carve(TILES * CW)
        pscr = carve(TILES * CW)
        cursor[0] = 0
        w13 = [[None, None], [None, None]]
        w2 = [None, None]
        for q in range(2):
            for j in range(2):
                w13[q][j] = carve(WCOLS).rearrange("p (c f) -> p c f", c=KT)
            w2[q] = carve(WCOLS).rearrange("p (c n) -> p c n", c=4)
        assert 3 * WCOLS <= HCOLS
        ygot = [[arena[:, (2 * t + j) * D:(2 * t + j + 1) * D] for j in range(2)] for t in range(TILES)]
        xg = [carve(D) for _ in range(2)]
        yo = [carve(D) for _ in range(2)]
        gidx = [carve(1).bitcast(I32) for _ in range(2)]
        flat = xT[:].rearrange("p k n -> p (k n)")
        xgT = [flat[:, q * D:(q + 1) * D].rearrange("p (c m) -> p c m", c=KT) for q in range(2)]
        hm = [flat[:, 2 * D + q * FF:2 * D + (q + 1) * FF] for q in range(2)]
        sg = hm
        hT = [flat[:, 2 * D + (2 + q) * FF:2 * D + (3 + q) * FF].rearrange("p (c m) -> p c m", c=4) for q in range(2)]
        cursor[0] = HCOLS
        R = carve(6144)
        EARLIER = 4096

        ps = [ctx.enter_context(nc.psum_tensor(f"ps{i}", [128, 512], F32)) for i in range(8)]

        x1d = io["x1d"]
        yd = io["yd"]

        def onehots(R):
            a = 2048
            place = R[:, a:a + 2 * TILES * 128].rearrange("p (k m) -> p k m", k=2 * TILES)
            b = a + 2 * TILES * 128
            whose = R[:, b:b + 2 * TILES * NI].rearrange("p (k m) -> p k m", k=2 * TILES)
            return place, whose

        class Eng:

            def __init__(self, eng, chain):
                self.e, self.chain, self.n, self.L = eng, chain, 0, 0

            def need(self, name, n):
                assert 0 < n <= PER[name], (name, n)
                self.e.wait_ge(sem(name), self.L * PER[name] + n)

            def done(self, ins, name, by=1):
                made[name] = made.get(name, 0) + by
                ins.then_inc(sem(name), by)
                return ins

            def link(self, ins):
                self.n += 1
                ins.then_inc(sem(self.chain + "_chain"), 1)
                self.e.wait_ge(sem(self.chain + "_chain"), self.n)

        start_sem = sem("start")
        block = ctx.enter_context(nc.Block())

        @block.sync
        def _(sp):
            E = Eng(sp, "none")
            sp.dma_start(const[:], io["const"]).then_inc(start_sem, 16)
            for t in range(TILES):
                sp.dma_start(x[0:ROWS[t], t, :], io["x_in"][128 * t:128 * t + ROWS[t], :]).then_inc(start_sem, 16)
            for L in range(DEPTH):
                E.L = L
                def ring_load(c):
                    if c >= 2:
                        E.need("proj" if c - 2 < NCH else "wout", (c - 1 if c - 2 < NCH else c - 1 - NCH) * TILES)
                    src = io["w_proj"][bass.ds(L * (NCH + NOUT) + c, 1), :, :].rearrange("a p n -> (a p) n")
                    sp.dma_start(ring[c % 2].rearrange("p k c -> p (k c)"), src).then_inc(sem(f"ring{c % 2}"), 16)

                def kv_load(i):
                    if i >= NKV:
                        E.need("kv_used", i - NKV + 1)
                    at = L * 2 * NB + i // NB * NB + CACHES[i % NB]
                    src = io["kv"][bass.ds(at, 1), :, :].rearrange("a p n -> (a p) n")
                    sp.dma_start(kv[i % NKV], src).then_inc(sem(f"kv{i % NKV}"), 16)

                for c in range(NCH):
                    ring_load(c)
                    if c == 1:
                        sp.wait_ge(sem("x2"), L * TILES)
                        E.done(sp.dma_start(rowpar[:], io["rowpar"][bass.ds(L * 128, 128), :]), "par_in", 16)
                        E.done(sp.dma_start(colpar[:], io["colpar"][bass.ds(L * 128, 128), :]), "par_in", 16)
                    if c < NKV - 1:
                        kv_load(c)
                for c in range(NCH, NCH + 2):
                    ring_load(c)
                E.need("conv_tr", 5)
                for i in range(NKV - 1, 2 * NB):
                    kv_load(i)
                E.need("glu", 1)
                out = io["p_conv"][bass.ds(L, 1)].rearrange("a p c -> (a p) c")
                E.done(sp.dma_start(out, h[128 - PAD:128, VAL, 3, :]), "stores", 16)
                out = io["s_conv"][bass.ds(L, 1)].rearrange("a p c -> (a p) c")
                E.done(sp.dma_start(out, h[0:NS, VAL, 4, :]), "stores", 16)
                E.need("sgu_vn", 1)
                out = io["s_sgu"][bass.ds(L, 1)].rearrange("a p c -> (a p) c")
                E.done(sp.dma_start(out, h[0:NS, V, 4, :]), "stores", 16)
                E.need("rot_s", 1)
                E.need("proj_out", 55)
                for name, s in (("k", SK), ("v", SV)):
                    out = io["p_" + name][bass.ds(L, 1)].rearrange("a (t p) c -> p (a t) c", p=128)
                    E.done(sp.dma_start(out, h[:, s, 0:4, :]), "stores", 16)
                out = io["s_k"][bass.ds(L, 1)].rearrange("a p c -> (a p) c")
                E.done(sp.dma_start(out, h[0:NS, SK, 4, :]), "stores", 16)
                out = io["s_v"][bass.ds(L, 1)].rearrange("a p c -> (a p) c")
                E.done(sp.dma_start(out, h[0:NS, SV, 4, :]), "stores", 16)
                E.need("ret_upd", 4)
                out = io["p_ret"][bass.ds(L, 1)].rearrange("a p n -> (a p) n")
                E.done(sp.dma_start(out, ret_S.rearrange("p c e -> p (c e)")), "stores", 16)
                E.need("smp_upd", 1)
                out = io["s_ret"][bass.ds(L, 1)].rearrange("a p n -> (a p) n")
                E.done(sp.dma_start(out, CP("ret_state")), "stores", 16)
                for c in range(NCH + 2, NCH + NOUT):
                    ring_load(c)
                E.need("stores", 16 * 9)
                E.need("xT_tr", 20)
                E.need("smp_back", 1)

                def expert_load(j, q, e):
                    src = io[("w1", "w3", "w2")[j]][bass.ds(L * NE + e, 1), :, :].rearrange("a p n -> (a p) n")
                    dst = (w13[q][j] if j < 2 else w2[q]).rearrange("p c n -> p (c n)")
                    sp.dma_start(dst, src).then_inc(sem(f"w{j}_{q}"), 16)

                for j in range(3):
                    expert_load(j, 0, 0)
                for t in range(TILES):
                    E.need("x1", t + 1)
                    E.done(sp.dma_start(x1d[128 * t:128 * t + ROWS[t], :], x[0:ROWS[t], t, :]), "x1_store", 16)
                E.need("routed", 1)
                lo = sp.value_load(trip[0:1, 0:1], min_val=1, max_val=1 + (DEPTH - 1) * NI // 2)
                turns = sp.value_load(trip[0:1, 1:2], min_val=NE // 2, max_val=NI // 2)

                for q in range(2):
                    sp.wait_ge(sem(f"xg{q}"), lo * 16)
                for j in range(3):
                    expert_load(j, 1, 1)
                used = ("w0_used", "w1_used", "y1_ps")
                with sp.Fori(1, turns) as turn:
                    i = sp.snap(lo + turn)
                    ea = sp.value_load(items[0:1, bass.ds(turn * 2, 1)], min_val=0, max_val=NE - 1)
                    eb = sp.value_load(items[0:1, bass.ds(turn * 2 + 1, 1)], min_val=0, max_val=NE - 1)
                    ra = sp.snap((ea + L * NE))
                    rb = sp.snap((eb + L * NE))
                    for j, q in ((0, 0), (1, 0), (0, 1), (1, 1), (2, 0), (2, 1)):
                        src = io[("w1", "w3", "w2")[j]][bass.ds((ra, rb)[q], 1), :, :].rearrange("a p n -> (a p) n")
                        dst = (w13[q][j] if j < 2 else w2[q]).rearrange("p c n -> p (c n)")
                        sp.wait_ge(sem(f"{used[j]}{q}"), i)
                        sp.dma_start(dst, src).then_inc(sem(f"w{j}_{q}"), 16)
                    for q in range(2):
                        row = sp.snap((turn - 1) * (2 * BLK) + q * BLK)
                        sp.wait_ge(sem(f"y_act{q}"), i)
                        sp.wait_ge(sem(f"y_dve{q}"), i)
                        sp.dma_start(yd[bass.ds(row, BLK), :], yo[q]).then_inc(sem(f"y_stored{q}"), 16)
                for q in range(2):
                    row = sp.snap((turns - 1) * (2 * BLK) + q * BLK)
                    sp.wait_ge(sem(f"y_act{q}"), lo + turns)
                    sp.wait_ge(sem(f"y_dve{q}"), lo + turns)
                    sp.dma_start(yd[bass.ds(row, BLK), :], yo[q]).then_inc(sem(f"y_stored{q}"), 16)
            for t in range(TILES):
                sp.wait_ge(sem("x2"), (DEPTH - 1) * PER["x2"] + t + 1)
                sp.dma_start(io["y"][128 * t:128 * t + ROWS[t], :], x[0:ROWS[t], t, :]).then_inc(sem("y_out"), 16)
            sp.wait_ge(sem("y_out"), 16 * TILES)

        @block.tensor
        def _(pe):
            E = Eng(pe, "none")
            ident = C("ident")
            pe.wait_ge(start_sem, 16 * (1 + TILES))
            for L in range(DEPTH):
                E.L = L
                turned = [0]

                def turn_rows(source, ready=None, use=None):
                    for t in range(TILES):
                        n = ROWS[t]
                        if ready:
                            ready(t)
                        for g in range(2):
                            k = turned[0]
                            if k >= 2:
                                E.need(("xT_low", "xT_high")[g], k // 2)
                            for j in range(4):
                                ins = pe.transpose(ps[g][:, j * 128:j * 128 + n], source(t, 4 * g + j), ident[0:n, 0:n])
                            E.done(ins, "xT_tr")
                            turned[0] += 1
                        if use and t:
                            use(t - 1)
                    if use:
                        use(TILES - 1)

                def x_block(t, k):
                    return x[0:ROWS[t], t, k * 128:(k + 1) * 128]

                def chunk(c, done, left, tiles=range(TILES)):
                    if 0 in tiles:
                        pe.wait_ge(sem(f"ring{c % 2}"), (L * (8 - c % 2) + c // 2 + 1) * 16)
                    for t in tiles:
                        n = ROWS[t]
                        j = (c if c < NCH else c - NCH) * TILES + t
                        if j >= TILES:
                            E.need(left, j - TILES + 1)
                        for k in range(KT):
                            if t < TILES - 1:
                                ins = pe.matmul(ps[2 + t][0:n, 0:CW], xT[:, k, 128 * t:128 * t + n], ring[c % 2][:, k, :],
                                                start=(k == 0), stop=(k == KT - 1))
                                continue
                            for j in range(4):
                                ins = pe.matmul(ps[2 + t][NS * j:NS * (j + 1), 0:QW], xT[:, k, SEQ:NTOK],
                                                ring[c % 2][:, k, j * QW:(j + 1) * QW], start=(k == 0), stop=(k == KT - 1),
                                                tile_position=(0, NS * j))
                        E.done(ins, done)

                def first_chunk(t):
                    E.need("xT_low", t + 1)
                    E.need("xT_high", t + 1)
                    chunk(0, "proj", "proj_out", [t])

                turn_rows(x_block, (lambda t: pe.wait_ge(sem("x2"), (L - 1) * TILES + t + 1)) if L else None, first_chunk)
                for c in range(1, 5):
                    chunk(c, "proj", "proj_out")
                E.need("glu", 1)
                for cb in range(2):
                    for t in range(4):
                        ins = pe.transpose(ps[cb][:, t * 128:(t + 1) * 128], h[:, VAL, t, cb * 128:(cb + 1) * 128], ident)
                    E.done(ins, "ctx_tr")
                E.need("ctx_out", 1)
                for cb in range(2):
                    ins = pe.transpose(ps[0][:, cb * NS:(cb + 1) * NS], h[0:NS, VAL, 4, cb * 128:(cb + 1) * 128],
                                       ident[0:NS, 0:NS])
                E.done(ins, "ctx_tr")
                for c in range(5, 9):
                    chunk(c, "proj", "proj_out")
                E.need("conv_done", 2)
                E.need("ctx_out", 3)
                for t in range(TILES):
                    n = ROWS[t]
                    if t >= 2:
                        E.need("conv_out", t - 1)
                    for cb in range(2):
                        src = acc[:, cb, 128 * t:128 * t + 128] if t < 4 else scr[:, cb * NS:(cb + 1) * NS]
                        ins = pe.transpose(ps[t % 2][0:n, cb * 128:(cb + 1) * 128], src, ident)
                    E.done(ins, "conv_tr")
                chunk(9, "proj", "proj_out")
                E.need("sgu_vn", 1)
                E.need("sgu_w", 1)
                wT = CP("sgu_wT").rearrange("p (g t) -> p g t", g=4)
                wTs = CP("sgu_wT_s").rearrange("p (g t) -> p g t", g=4)
                E.need("conv_out", 5)
                for g in range(4):
                    ins = pe.matmul(ps[(7, 0)[g // 2]][:, (g % 2) * 256:(g % 2) * 256 + 256], wT[:, g, :],
                                    h[:, V, 0:4, g * 64:(g + 1) * 64], start=True, stop=True)
                    if g % 2:
                        E.done(ins, "sgu_z")
                for g in range(4):
                    ins = pe.matmul(ps[1][0:NS, g * 64:(g + 1) * 64], wTs[0:NS, g, :], h[0:NS, V, 4, g * 64:(g + 1) * 64],
                                    start=True, stop=True)
                E.done(ins, "sgu_z")
                chunk(10, "proj", "proj_out")
                E.need("rot_r", 1)
                E.need("rot_s", 1)
                E.need("sgu_y", 1)
                order = [(s, hp) for s in (RQ, RK, SQ, SK) for hp in range(2)]
                for k, (s, hp) in enumerate(order):
                    if k >= 2:
                        E.need(("qk_act", "qk_dve")[k % 2], k // 2)
                    for t in range(4):
                        ins = pe.transpose(ps[k % 2][:, t * 128:(t + 1) * 128], h[:, s, t, hp * 128:(hp + 1) * 128], ident)
                    E.done(ins, "qk_tr")
                E.need("qk_act", 4)
                for k, (s, hp) in enumerate(order):
                    ins = pe.transpose(ps[0][:, k * NS:(k + 1) * NS], h[0:NS, s, 4, hp * 128:(hp + 1) * 128],
                                       ident[0:NS, 0:NS])
                E.done(ins, "qk_tr")
                E.need("qk_act", 5)
                E.need("qk_dve", 4)
                E.need("proj_out", 55)

                def half(hh):
                    return slice(64 * hh, 64 * hh + 64)

                def ret_scores(n):
                    if n >= 2:
                        E.need("ret_a", n - 1)
                    for hd in range(NH):
                        hp, hh = hd // 2, hd % 2
                        b = ps[((2, 5), (6, 7))[n % 2][hh]]
                        ins = pe.matmul(b[:, hp * 128:(hp + 1) * 128], xT[half(hh), 2 + hp, n * 128:(n + 1) * 128],
                                        xT[half(hh), hp, n * 128:(n + 1) * 128], start=True, stop=True)
                    E.done(ins, "ret_s")

                def ret_products(n):
                    for hp in range(2):
                        ins = pe.matmul(ps[(4, 0)[n % 2]][:, hp * 128:(hp + 1) * 128], h[:, RK, n, hp * 128:(hp + 1) * 128],
                                        h[:, RV, n, hp * 128:(hp + 1) * 128], start=True, stop=True)
                    E.done(ins, "ret_kv")

                ret_scores(0)
                ret_scores(1)
                E.need("k_dec", 1)
                ret_products(0)
                for n in range(4):
                    E.need("ret_a", n + 1)
                    if n:
                        E.need("ret_upd", n)
                    for hd in range(NH):
                        hp, hh = hd // 2, hd % 2
                        o = ps[(3, 1)[hh]][:, hp * HD:(hp + 1) * HD]
                        ins = pe.matmul(o, pT[n % 2][:, hd * 128:(hd + 1) * 128],
                                        h[:, RV, n, hd * HD:(hd + 1) * HD], start=True, stop=(n == 0))
                        if n:
                            ins = pe.matmul(o, xT[half(hh), hp, n * 128:(n + 1) * 128],
                                            ret_S[half(hh), hp, :], start=False, stop=True)
                    E.done(ins, "ret_o")
                    if n < 3:
                        ret_products(n + 1)
                    if n < 2:
                        ret_scores(n + 2)
                s0 = CP("ret_state").rearrange("p (c b e) -> p c b e", c=2, b=NB)
                for hd in range(NH):
                    hp, hh = hd // 2, hd % 2
                    ins = pe.matmul(ps[(2, 5)[hh]][0:NS, hp * NS:(hp + 1) * NS], xT[half(hh), 2 + hp, SEQ:NTOK],
                                    xT[half(hh), hp, SEQ:NTOK], start=True, stop=True)
                E.done(ins, "ret_s")
                for hp in range(2):
                    for b, hh in np.ndindex(NB, 2):
                        ins = pe.matmul(ps[6 + hh][0:64, hp * NS + b * NT:hp * NS + (b + 1) * NT], s0[half(hh), hp, b, :],
                                        xT[half(hh), hp, SEQ + b * NT:SEQ + (b + 1) * NT], start=True, stop=True)
                E.done(ins, "smp_o1")
                E.need("ret_a", 5)
                E.need("smp_o1c", 1)
                E.need("ret_upd", 4)
                for hd in range(NH):
                    pe.matmul(ps[3][0:NS, hd * HD:(hd + 1) * HD], sm[0][0:NS, hd * NS:(hd + 1) * NS],
                              h[0:NS, RV, 4, hd * HD:(hd + 1) * HD], start=True, stop=False)
                    ins = pe.matmul(ps[3][0:NS, hd * HD:(hd + 1) * HD], sm[1][0:64, hd * NS:(hd + 1) * NS],
                                    ident[0:64, 0:64], start=False, stop=True)
                E.need("vexp", 1)
                for hd in range(NH):
                    hp, hh = hd // 2, hd % 2
                    ins = pe.matmul(ps[4 + hp][half(hh), :], h[0:NS, RK, 4, hd * HD:(hd + 1) * HD],
                                    vexp[:, hd, :, :].rearrange("p b e -> p (b e)"), start=True, stop=True)
                E.done(ins, "smp_o")

                def att_scores(u):
                    i, hd = u // 4, u % 4
                    hp, hh = hd // 2, hd % 2
                    b = ps[2] if u % 2 == 0 else ps[5]
                    if u >= 2:
                        E.need("att_m", u - 1)
                    n = (i + 1) * 128
                    ins = pe.matmul(b[:, 0:n], xT[half(hh), 4 + hp, i * 128:(i + 1) * 128], xT[half(hh), 6 + hp, 0:n],
                                    start=True, stop=True)
                    E.done(ins, "att_s")

                def kv_wait(i):
                    uses = len(range(i % NKV, 16, NKV))
                    pe.wait_ge(sem(f"kv{i % NKV}"), (L * uses + i // NKV + 1) * 16)

                def new_key_scores():
                    for b in range(NB):
                        rows = slice(32 * (b // 2), 32 * (b // 2) + 32)
                        for hp in range(2):
                            pe.matmul(ps[1][rows, 128:128 + NS], QB[:, hp, 32 * b:32 * b + 32], xT[:, 6 + hp, SEQ:NTOK],
                                      start=(b % 2 == 0 and hp == 0), stop=(b % 2 == 1 and hp == 1),
                                      tile_position=(0, 32 * (b // 2)))

                def cached_key_scores(i):
                    kv_wait(i)
                    kv_wait(i + 1)
                    for hp in range(2):
                        for bank, a, n in ((0, 0, 512), (1, 512, 128)):
                            for j in (i, i + 1):
                                b = CACHES[j]
                                rows = slice(32 * (b // 2), 32 * (b // 2) + 32)
                                kb = kv[j % NKV].rearrange("p (c k) -> p c k", c=2)
                                ins = pe.matmul(ps[bank][rows, 0:n], QB[:, hp, 32 * b:32 * b + 32], kb[:, hp, a:a + n],
                                                start=(b % 2 == 0 and hp == 0), stop=(b % 2 == 1 and hp == 1),
                                                tile_position=(0, 32 * (b // 2)))
                                if hp == 1 and bank == 1:
                                    E.done(ins, "kv_used")

                def turn_sample_probs():
                    E.need("smp_n", 1)
                    for k in range(4):
                        pe.transpose(ps[0][:, k * 128:(k + 1) * 128], ss[:, k * 128:(k + 1) * 128], ident)
                    pe.transpose(ps[1][:, 0:128], ss[:, 512:640], ident)
                    E.done(pe.transpose(ps[1][0:NS, 128:256], ss[:, 640:672], ident), "smp_t")

                def sample_values(i):
                    E.need("smp_pT", 1)
                    kv_wait(NB + i)
                    kv_wait(NB + i + 1)
                    for k in range(6):
                        for j in (i, i + 1):
                            b = CACHES[j]
                            rows = slice(32 * (b // 2), 32 * (b // 2) + 32)
                            vb = kv[(NB + j) % NKV].rearrange("p (k c) -> p k c", k=5)
                            o = ps[0][rows, b % 2 * 256:b % 2 * 256 + 256]
                            pos = (0, 32 * (b // 2))
                            if k < 5:
                                pe.matmul(o, PTs[:, k, rows], vb[:, k, :], start=(k == 0), stop=False, tile_position=pos)
                            else:
                                E.done(pe.matmul(o, PTs[0:NS, 5, rows], h[0:NS, SV, 4, :], start=False, stop=True,
                                                 tile_position=pos), "kv_used")

                def att_values(u):
                    i, hd = u // 4, u % 4
                    E.need("att_pT", u + 1)
                    if u >= 2:
                        E.need("att_y", u - 1)
                    bo = ps[4] if u % 2 == 0 else ps[7]
                    for k in range(i + 1):
                        ins = pe.matmul(bo[:, 0:HD], pT[u % 2][:, k * 128:(k + 1) * 128], h[:, SV, k, hd * HD:(hd + 1) * HD],
                                        start=(k == 0), stop=(k == i))
                    E.done(ins, "att_o")

                E.need("qb_ok", 1)
                new_key_scores()
                E.need("smp_upd", 1)
                att_scores(0)
                for u in range(16):
                    i, hd = u // 4, u % 4
                    if u < 15:
                        att_scores(u + 1)
                    E.need("att_p", u + 1)
                    if u >= 2:
                        E.need("att_pT", u - 1)
                    bt = ps[3] if u % 2 == 0 else ps[6]
                    for k in range(i + 1):
                        ins = pe.transpose(bt[:, k * 128:(k + 1) * 128], sm[u % 2][:, k * 128:(k + 1) * 128], ident)
                    E.done(ins, "att_t")
                    if u in (0, 2, 4, 6):
                        cached_key_scores(u)
                    if u == 10:
                        turn_sample_probs()
                    if u in (11, 12, 13, 14):
                        sample_values(2 * (u - 11))
                    if u:
                        att_values(u - 1)
                att_values(15)
                E.need("att_y", 16)
                E.need("smp_rows", 1)
                for hd in range(NH):
                    ins = pe.matmul(ps[5][0:NS, hd * HD:(hd + 1) * HD], C("pick")[:, hd * NS:(hd + 1) * NS],
                                    sm[0][:, hd * HD:(hd + 1) * HD], start=True, stop=True)
                E.done(ins, "smp_back")

                E.need("smp_y", 1)
                E.need("ret_y", 1)
                E.need("conv_y", 1)
                mix = [RQ, SQ, GATE, U]
                turn_rows(lambda t, k: h[0:ROWS[t], mix[k // 2], t, (k % 2) * 128:(k % 2) * 128 + 128])
                E.need("xT_low", 10)
                E.need("xT_high", 10)
                for c in range(NCH, NCH + NOUT):
                    chunk(c, "wout", "wout_out")
                rw = CP("router_w").rearrange("p (k n) -> p k n", k=KT)

                def tile_logits(t):
                    n = ROWS[t]
                    E.need("xT_low", 2 * TILES + t + 1)
                    E.need("xT_high", 2 * TILES + t + 1)
                    if t == 0:
                        E.need("wout_out", 16)
                    for k in range(KT):
                        ins = pe.matmul(ps[2][0:n, t * 36:t * 36 + 36], xT[:, k, 128 * t:128 * t + n], rw[:, k, :],
                                        start=(k == 0), stop=(k == KT - 1))
                    if t == TILES - 1:
                        E.done(ins, "logits")

                turn_rows(x_block, lambda t: E.need("x1", t + 1), tile_logits)
                E.need("member", 1)
                earlier = R[:, EARLIER:EARLIER + (TILES + 1) * NE]
                E.done(pe.matmul(ps[4][:, 0:NE], C("ones"), earlier[:, TILES * NE:], start=True, stop=True), "counts")
                pe.matmul(ps[3][:, 0:TILES * NE], C("before"), R[:, 0:TILES * NE], start=True, stop=False)
                ins = pe.matmul(ps[3][:, 0:TILES * NE], C("ones"), earlier[:, 0:TILES * NE], start=False, stop=True)
                E.done(ins, "places")
                E.need("onehot", 1)
                place, whose = onehots(R)
                for k in range(2 * TILES):
                    ins = pe.matmul(ps[5][:, 0:NI], place[:, k, :], whose[:, k, :], start=(k == 0), stop=(k == 2 * TILES - 1))
                E.done(ins, "idx_ps")
                E.need("routed", 1)
                lo = pe.value_load(trip[0:1, 0:1], min_val=1, max_val=1 + (DEPTH - 1) * NI // 2)
                turns = pe.value_load(trip[0:1, 1:2], min_val=NE // 2, max_val=NI // 2)
                with pe.Fori(0, turns) as turn:
                    i = pe.snap(lo + turn)
                    for q in range(2):
                        pe.wait_ge(sem(f"xg{q}"), i * 16)
                        v = xg[q].rearrange("p (k c) -> p c k", c=KT)
                        for g in range(2):
                            if q:
                                pe.wait_ge(sem(("xgT_act0", "xgT_dve0")[g]), i + 1)
                            for c in range(4):
                                ins = pe.transpose(ps[g][:, c * BLK:(c + 1) * BLK], v[:, 4 * g + c, :], ident)
                            ins.then_inc(sem(f"xg_tr{g}_{q}"), 1)
                    for q in range(2):
                        pe.wait_ge(sem(f"xgT_act{q}"), i + 1)
                        pe.wait_ge(sem(f"xgT_dve{q}"), i + 1)
                        for j in range(2):
                            pe.wait_ge(sem(f"w{j}_{q}"), (i + 1) * 16)
                            pe.wait_ge(sem(f"hm{q}"), i)
                            for c in range(KT):
                                ins = pe.matmul(ps[2 + 2 * q + j][0:BLK, :], xgT[q][:, c, :], w13[q][j][:, c, :],
                                                start=(c == 0), stop=(c == KT - 1))
                            ins.then_inc(sem(f"w{j}_used{q}"), 1)
                    for q in range(2):
                        pe.wait_ge(sem(f"hm{q}"), i + 1)
                        v = hm[q].rearrange("p (f c) -> p c f", c=4)
                        for c in range(4):
                            ins = pe.transpose(ps[q][:, c * BLK:(c + 1) * BLK], v[:, c, :], ident)
                        ins.then_inc(sem(f"hm_tr{q}"), 1)
                        pe.wait_ge(sem(f"hT{q}"), i + 1)
                        pe.wait_ge(sem(f"w2_{q}"), (i + 1) * 16)
                        if q:
                            pe.wait_ge(sem("y_act0"), i + 1)
                            pe.wait_ge(sem("y_dve0"), i + 1)
                        else:
                            pe.wait_ge(sem("y_act1"), i)
                            pe.wait_ge(sem("y_dve1"), i)
                        for n in range(2):
                            for c in range(4):
                                ins = pe.matmul(ps[6 + n][0:BLK, :], hT[q][:, c, :], w2[q][:, c, n * 512:(n + 1) * 512],
                                                start=(c == 0), stop=(c == 3))
                            ins.then_inc(sem(f"y{n}_ps{q}"), 1)

        @block.scalar
        def _(act):
            E = Eng(act, "act")
            act.wait_ge(start_sem, 16 * (1 + TILES))
            act.wait_ge(sem("pinit"), 2)
            for L in range(DEPTH):
                E.L = L
                turned = [0]

                def turn_out(banks):
                    for t in range(TILES):
                        n = ROWS[t]
                        for g in banks:
                            E.need("xT_tr", 2 * turned[0] + 1 + g)
                            src = ps[g][:, :].rearrange("p (j m) -> p j m", j=4)[:, :, 0:n]
                            E.done(act.copy(xT[:, 4 * g:4 * g + 4, 128 * t:128 * t + n], src), ("xT_low", "xT_high")[g])
                        turned[0] += 1

                turn_out((0, 1))
                func = {GATE: ACT.Sigmoid, U: ACT.Gelu_apprx_tanh, V: ACT.Gelu_apprx_tanh, RG: ACT.Silu}
                for c in range(NCH):
                    for t in range(TILES):
                        n = ROWS[t]
                        E.need("proj", c * TILES + t + 1)
                        if t < TILES - 1:
                            ins = act.activation(h[0:n, c, t, :], ps[2 + t][0:n, 0:CW], func.get(c, ACT.Copy))
                        else:
                            for j in range(4):
                                ins = act.activation(h[0:n, c, t, j * QW:(j + 1) * QW], ps[2 + t][NS * j:NS * (j + 1), 0:QW],
                                                     func.get(c, ACT.Copy))
                        E.done(ins, "proj_out")
                E.need("conv_norm", 1)
                E.done(act.activation(h[:, GATE], h[:, GATE], ACT.Silu), "conv_y")
                for k in range(0, 8, 2):
                    E.need("qk_tr", k + 1)
                    E.done(act.copy(xT[:, k, 0:SEQ], ps[0][:, :]), "qk_act")
                E.need("qk_tr", 9)
                E.done(act.copy(xT[:, 0:8, SEQ:NTOK], ps[0][:, 0:8 * NS].rearrange("p (k n) -> p k n", k=8)), "qk_act")
                E.need("smp_o1", 1)
                for hh in range(2):
                    dst = sm[1][0:64, 0:NH * NS].rearrange("p (c g n) -> p c g n", c=2, g=2)[:, :, hh, :]
                    ins = act.copy(dst, ps[6 + hh][0:64, 0:2 * NS].rearrange("p (c n) -> p c n", c=2))
                E.done(ins, "smp_o1c")
                for u in range(16):
                    n = (u // 4 + 1) * 128
                    E.need("att_m", u + 1)
                    E.done(act.activation(sm[u % 2][:, 0:n], sm[u % 2][:, 0:n], ACT.Exp, bias=small[:, u % 2:u % 2 + 1],
                                          accum_out=small[:, 2 + u % 2:3 + u % 2]), "att_p")
                    E.need("att_t", u + 1)
                    if u >= 2:
                        E.need("att_o", u - 1)
                    bt = ps[3] if u % 2 == 0 else ps[6]
                    E.done(act.copy(pT[u % 2][:, 0:n], bt[:, 0:n]), "att_pT")
                    if u == 8:
                        E.need("smp_m", 1)
                        E.done(act.activation(ss, ss, ACT.Exp, bias=small[:, 4:5], accum_out=small[:, 5:6]), "smp_p")
                    if u == 10:
                        E.need("smp_t", 1)
                        E.link(act.copy(PTs[:, 0:4, :], ps[0][:, :].rearrange("p (k r) -> p k r", k=4)))
                        E.link(act.copy(PTs[:, 4, :], ps[1][:, 0:128]))
                        E.done(act.copy(PTs[0:NS, 5, :], ps[1][0:NS, 128:256]), "smp_pT")
                turn_out((0,))
                turn_out((0, 1))
                E.need("ex_in", 1)
                ex = R[:, 400:400 + TILES * NG]
                E.done(act.activation(ex, ex, ACT.Exp), "ex_out")
                E.need("ex2_in", 1)
                ex2 = R[:, 440:440 + TILES]
                E.done(act.activation(ex2, ex2, ACT.Exp), "ex2_out")
                E.need("routed", 1)
                lo = act.value_load(trip[0:1, 0:1], min_val=1, max_val=1 + (DEPTH - 1) * NI // 2)
                turns = act.value_load(trip[0:1, 1:2], min_val=NE // 2, max_val=NI // 2)
                with act.Fori(0, turns) as turn:
                    i = act.snap(lo + turn)
                    for q in range(2):
                        act.wait_ge(sem(f"xg_tr0_{q}"), i + 1)
                        act.copy(xgT[q][:, 0:4, :], ps[0][:, 0:4 * BLK].rearrange("p (c m) -> p c m", c=4))\
                           .then_inc(sem(f"xgT_act{q}"), 1)
                    for q in range(2):
                        act.wait_ge(sem(f"w0_used{q}"), i + 1)
                        act.activation(sg[q], ps[2 + 2 * q][0:BLK, :], ACT.Silu).then_inc(sem(f"sg{q}"), 1)
                    for q in range(2):
                        act.wait_ge(sem(f"hm_tr{q}"), i + 1)
                        act.copy(hT[q], ps[q][:, 0:4 * BLK].rearrange("p (c m) -> p c m", c=4)).then_inc(sem(f"hT{q}"), 1)
                        act.wait_ge(sem(f"y0_ps{q}"), i + 1)
                        act.wait_ge(sem(f"y_stored{q}"), i * 16)
                        act.copy(yo[q][:, 0:512], ps[6][0:BLK, :]).then_inc(sem(f"y_act{q}"), 1)

        @block.vector
        def _(dve):
            E = Eng(dve, "dve")
            dve.memset(cum[:], 1.0).then_inc(sem("init"), 1)
            dve.wait_ge(sem("init"), 1)
            dve.wait_ge(start_sem, 16 * (1 + TILES))

            def group_norm(rows, groups, size, stat, gain, bias, out):
                n = TILES * groups
                r3 = rows.rearrange("p t (g c) -> p (t g) c", c=size)
                s3 = scr[:, 0:n * size].rearrange("p (a c) -> p a c", c=size)
                mean, var = stat[:, 0:n], stat[:, n:2 * n]
                E.link(dve.tensor_reduce(mean, r3, AX, ALU.add))
                E.link(dve.tensor_scalar(mean, mean, 1.0 / size, None, ALU.mult))
                E.link(dve.tensor_tensor(r3, r3, mean.unsqueeze(2).to_broadcast([128, n, size]), ALU.subtract))
                E.link(dve.tensor_tensor(s3, r3, r3, ALU.mult))
                E.link(dve.tensor_reduce(var, s3, AX, ALU.add))
                E.done(dve.tensor_scalar(var, var, 1.0 / size, EPS, ALU.mult, ALU.add), "st_in")
                stat_n[0] += 1
                E.need("st_out", stat_n[0])
                E.link(dve.tensor_tensor(r3, r3, var.unsqueeze(2).to_broadcast([128, n, size]), ALU.mult))
                g4 = gain.unsqueeze(1).to_broadcast([128, TILES, groups * size])
                ins = dve.tensor_tensor(out, rows, g4, ALU.mult)
                if bias is not None:
                    E.link(ins)
                    ins = dve.tensor_tensor(out, out, bias.unsqueeze(1).to_broadcast([128, TILES, groups * size]), ALU.add)
                return ins

            for L in range(DEPTH):
                E.L = L
                stat_n = [0]
                stats = pstat

                E.need("proj_out", (V + 1) * TILES)
                E.done(group_norm(h[:, V], 4, 64, stats, RP("sgu_ln_g"), RP("sgu_ln_b"), h[:, V]), "sgu_vn")
                E.need("ctx_pool", 1)
                for cb in range(2):
                    E.need("ctx_tr", cb + 1)
                    E.done(dve.tensor_copy(ctxb[:, cb, PAD:SAMP0], ps[cb][:, :]), "ctx_out")
                E.need("ctx_tr", 3)
                smp = ctxb[:, :, SAMP0:CTXW].rearrange("p c (b w) -> p c b w", b=NB)
                for cb in range(2):
                    src = ps[0][:, cb * NS:(cb + 1) * NS].rearrange("p (b t) -> p b t", b=NB)
                    ins = dve.tensor_copy(smp[:, cb, :, PAD:PAD + NT], src)
                    if cb == 0:
                        E.link(ins)
                E.done(ins, "ctx_out")
                E.need("ctx_out", 3)
                cw, cbias = CP("conv_w"), CP("conv_b")
                for j in range(TAPS):
                    for cb in range(2):
                        src = ctxb[:, cb, j:j + ACCW]
                        if j == 0:
                            ins = dve.tensor_scalar(acc[:, cb, :], src, cw[:, cb * TAPS:cb * TAPS + 1], cbias[:, cb:cb + 1],
                                                    ALU.mult, ALU.add)
                        else:
                            ins = dve.scalar_tensor_tensor(out=acc[:, cb, :], in0=src, scalar=cw[:, cb * TAPS + j:cb * TAPS + j + 1],
                                                           in1=acc[:, cb, :], op0=ALU.mult, op1=ALU.add)
                        E.n += 1
                        ins.then_inc(sem("dve_chain"), 1)
                        if E.n > 1:
                            dve.wait_ge(sem("dve_chain"), E.n - 1)
                dve.wait_ge(sem("dve_chain"), E.n)
                for cb in range(2):
                    for b in range(NB):
                        a = SAMP0 + b * (PAD + NT)
                        ins = dve.tensor_copy(scr[:, cb * NS + b * NT:cb * NS + (b + 1) * NT], acc[:, cb, a:a + NT])
                    E.done(ins, "conv_done")
                E.need("conv_done", 2)
                for t in range(TILES):
                    n = ROWS[t]
                    E.need("conv_tr", t + 1)
                    E.done(dve.tensor_copy(h[0:n, GATE, t, :], ps[t % 2][0:n, 0:256]), "conv_out")
                E.need("conv_out", 5)
                E.done(group_norm(h[:, GATE], 1, 256, stats, RP("conv_ln_g"), RP("conv_ln_b"), h[:, GATE]), "conv_norm")
                for g in range(4):
                    if g % 2 == 0:
                        E.need("sgu_z", g // 2 + 1)
                    uu = h[:, U, 0:4, g * 64:(g + 1) * 64]
                    z = ps[(7, 0)[g // 2]][:, (g % 2) * 256:(g % 2) * 256 + 256].rearrange("p (t c) -> p t c", t=4)
                    dve.scalar_tensor_tensor(out=uu, in0=z, scalar=CP("sgu_b")[:, g:g + 1], in1=uu, op0=ALU.add, op1=ALU.mult)
                E.need("sgu_z", 3)
                for g in range(4):
                    uu = h[0:NS, U, 4, g * 64:(g + 1) * 64]
                    ins = dve.scalar_tensor_tensor(out=uu, in0=ps[1][0:NS, g * 64:(g + 1) * 64],
                                                   scalar=CP("sgu_b_s")[0:NS, g:g + 1], in1=uu, op0=ALU.add, op1=ALU.mult)
                E.done(ins, "sgu_y")
                for k in range(1, 8, 2):
                    E.need("qk_tr", k + 1)
                    E.done(dve.tensor_copy(xT[:, k, 0:SEQ], ps[1][:, :]), "qk_dve")
                E.link(dve.memset(ret_S, 0.0))
                mask = C("ret_mask")
                qd = C("q_decay").rearrange("p (t h) -> p t h", t=TILES)

                def mask_scores(n):
                    E.need("ret_s", n + 1)
                    if n >= 2:
                        E.need("ret_o", n - 1)
                    for hh in range(2):
                        b = ps[((2, 5), (6, 7))[n % 2][hh]]
                        dst = pT[n % 2].rearrange("p (c g k) -> p c g k", c=2, g=2)[:, :, hh, :]
                        m = mask.rearrange("p (c g k) -> p c g k", c=2, g=2)[:, :, hh, :]
                        ins = dve.tensor_tensor(dst, b[:, 0:256].rearrange("p (c k) -> p c k", c=2), m, ALU.mult)
                    E.done(ins, "ret_a")

                mask_scores(0)
                mask_scores(1)
                for n in range(4):
                    E.need("ret_o", n + 1)
                    E.need("ret_kv", n + 1)
                    for hh in range(2):
                        dst = h[:, RQ, n, :].rearrange("p (c g e) -> p c g e", c=2, g=2)[:, :, hh, :]
                        dec = qd[:, n, :].rearrange("p (c g) -> p c g", c=2)[:, :, hh]
                        dve.tensor_tensor(dst, ps[(3, 1)[hh]][:, 0:128].rearrange("p (c e) -> p c e", c=2),
                                          dec.unsqueeze(2).to_broadcast([128, 2, HD]), ALU.mult)
                    for hp in range(2):
                        for hh in range(2):
                            r = slice(64 * hh, 64 * hh + 64)
                            ins = dve.scalar_tensor_tensor(out=ret_S[r, hp, :], in0=ret_S[r, hp, :], scalar=C("c_decay")[r, hp:hp + 1],
                                                           in1=ps[(4, 0)[n % 2]][r, hp * 128 + hh * 64:hp * 128 + hh * 64 + 64],
                                                           op0=ALU.mult, op1=ALU.add)
                    E.done(ins, "ret_upd")
                    E.need("ret_upd", n + 1)
                    if n < 2:
                        mask_scores(n + 2)
                E.need("ret_s", 5)
                for hh in range(2):
                    dst, m = (z[0:NS, 0:NH * NS].rearrange("p (c g k) -> p c g k", c=2, g=2)[:, :, hh, :]
                              for z in (sm[0], C("ret_mask_s")))
                    ins = dve.tensor_tensor(dst, ps[(2, 5)[hh]][0:NS, 0:2 * NS].rearrange("p (c k) -> p c k", c=2), m, ALU.mult)
                E.done(ins, "ret_a")
                E.need("smp_o", 1)
                dve.tensor_tensor(h[0:NS, RQ, 4, :].rearrange("p (h c) -> p h c", h=NH),
                                  ps[3][0:NS, 0:256].rearrange("p (h c) -> p h c", h=NH),
                                  qd[0:NS, 4, :].unsqueeze(2).to_broadcast([NS, NH, HD]), ALU.mult)
                s0 = CP("ret_state").rearrange("p (c n) -> p c n", c=2)
                for hp in range(2):
                    ins = dve.scalar_tensor_tensor(out=s0[:, hp, :], in0=s0[:, hp, :], scalar=C("c_decay_s")[:, hp:hp + 1],
                                                   in1=ps[4 + hp][:, :], op0=ALU.mult, op1=ALU.add)
                E.done(ins, "smp_upd")
                E.need("smp_upd", 1)

                def attend(u):
                    i = u // 4
                    n = (i + 1) * 128
                    E.need("att_s", u + 1)
                    if u >= 2:
                        E.need("att_t", u - 1)
                    b = ps[2] if u % 2 == 0 else ps[5]
                    E.link(dve.scalar_tensor_tensor(out=sm[u % 2][:, 0:n], in0=b[:, 0:n], scalar=SCALE,
                                                    in1=C("attn_bias")[:, (3 - i) * 128:512], op0=ALU.mult, op1=ALU.add))
                    E.link(dve.tensor_reduce(small[:, 8 + u % 2:9 + u % 2], sm[u % 2][:, 0:n], AX, ALU.max))
                    E.done(dve.tensor_scalar(small[:, u % 2:u % 2 + 1], small[:, 8 + u % 2:9 + u % 2], -1.0, None, ALU.mult), "att_m")

                ng = TILES * NH
                mean, var = stats[:, 0:ng], stats[:, ng:2 * ng]

                def ret_norm_step(u):
                    if u == 0:
                        E.link(dve.tensor_reduce(mean, h[:, RQ].rearrange("p t (g c) -> p (t g) c", c=HD), AX, ALU.add))
                        E.done(dve.tensor_scalar(mean, mean, 1.0 / HD, None, ALU.mult), "ret_mean")
                    if u == 5:
                        E.need("ret_sq", 1)
                        squares = pscr[:, 0:ng * HD].rearrange("p (a c) -> p a c", c=HD)
                        E.link(dve.tensor_reduce(var, squares, AX, ALU.add))
                        E.done(dve.tensor_scalar(var, var, 1.0 / HD, EPS, ALU.mult, ALU.add), "st_in")

                def total_inverse(u):
                    E.need("att_p", u + 1)
                    E.link(dve.reciprocal(small[:, 10 + u % 2:11 + u % 2], small[:, 2 + u % 2:3 + u % 2]))

                def att_rows(u):
                    i, hd = u // 4, u % 4
                    E.need("att_o", u + 1)
                    bo = ps[4] if u % 2 == 0 else ps[7]
                    E.done(dve.tensor_scalar(h[:, SQ, i, hd * HD:(hd + 1) * HD], bo[:, 0:HD], small[:, 10 + u % 2:11 + u % 2],
                                             None, ALU.mult), "att_y")

                attend(0)
                for u in range(16):
                    if u:
                        total_inverse(u - 1)
                    if u < 15:
                        attend(u + 1)
                    ret_norm_step(u)
                    if u == 7:
                        E.need("kv_used", NB)
                        sbias = C("sample_bias")
                        for a, n, b in ((0, 512, ps[0][:, 0:512]), (512, 128 + NS, ps[1][:, 0:128 + NS])):
                            E.link(dve.scalar_tensor_tensor(out=ss[:, a:a + n], in0=b, scalar=SCALE, in1=sbias[:, a:a + n],
                                                            op0=ALU.mult, op1=ALU.add))
                        E.link(dve.tensor_reduce(small[:, 6:7], ss, AX, ALU.max))
                        E.done(dve.tensor_scalar(small[:, 4:5], small[:, 6:7], -1.0, None, ALU.mult), "smp_m")
                    if u == 9:
                        E.need("smp_p", 1)
                        E.link(dve.reciprocal(small[:, 7:8], small[:, 5:6]))
                        E.done(dve.tensor_scalar(ss, ss, small[:, 7:8], None, ALU.mult), "smp_n")
                    if u:
                        att_rows(u - 1)
                total_inverse(15)
                att_rows(15)
                E.need("kv_used", 16)
                par = C("parity")
                E.link(dve.tensor_scalar(sm[0][:, 0:256], ps[0][:, 0:256], par[:, 0:1], None, ALU.mult))
                E.done(dve.scalar_tensor_tensor(out=sm[0][:, 0:256], in0=ps[0][:, 256:512], scalar=par[:, 1:2],
                                                in1=sm[0][:, 0:256], op0=ALU.mult, op1=ALU.add), "smp_rows")
                E.need("smp_back", 1)
                E.done(dve.tensor_copy(h[0:NS, SQ, 4, :], ps[5][0:NS, 0:256]), "smp_y")
                for t in range(TILES):
                    n = ROWS[t]
                    E.need("xT_tr", 2 * (TILES + t) + 2)
                    src = ps[1][:, :].rearrange("p (j m) -> p j m", j=4)[:, :, 0:n]
                    E.done(dve.tensor_copy(xT[:, 4:8, 128 * t:128 * t + n], src), "xT_high")
                def half_stats(t, k):
                    n = ROWS[t]
                    return dve.bn_stats(bn[0:n, t, k, :], x[0:n, t, k * 512:(k + 1) * 512])

                def row_norm(t, gain, bias, pow_done, done):
                    n = ROWS[t]
                    xs = x[0:n, t, :]
                    E.link(dve.scalar_tensor_tensor(out=xs, in0=xs, scalar=mv[0:n, t, 0:1], in1=RP(gain)[0:n, :],
                                                    op0=ALU.subtract, op1=ALU.mult))
                    E.need(pow_done, t + 1)
                    E.done(dve.scalar_tensor_tensor(out=xs, in0=xs, scalar=mv[0:n, t, 2:3], in1=RP(bias)[0:n, :],
                                                    op0=ALU.mult, op1=ALU.add), done)

                for c in range(NOUT):
                    for t in range(TILES):
                        n = ROWS[t]
                        if c == 2:
                            E.need("wout_out", TILES + t + 1)
                            half_stats(t, 0)
                        E.need("wout", c * TILES + t + 1)
                        xs = x[0:n, t, c * CW:(c + 1) * CW]
                        mixed = ps[2 + t][0:n, 0:CW]
                        if t == TILES - 1:
                            mixed = scr[0:NS, 0:CW]
                            for j in range(4):
                                ins = dve.tensor_copy(mixed[:, j * QW:(j + 1) * QW], ps[2 + t][NS * j:NS * (j + 1), 0:QW])
                            E.link(ins)
                        E.done(dve.scalar_tensor_tensor(out=xs, in0=xs, scalar=ALPHA, in1=mixed,
                                                        op0=ALU.mult, op1=ALU.add), "wout_out")
                        if c == 3:
                            E.need("wout_out", 3 * TILES + t + 1)
                            E.link(half_stats(t, 1))
                            E.link(dve.bn_aggr(mv[0:n, t, 0:2], bn[0:n, t, :, :]))
                            E.done(dve.tensor_scalar(mv[0:n, t, 3:4], mv[0:n, t, 1:2], EPS, None, ALU.add), "x1_stat")
                            if t:
                                row_norm(t - 1, "ln1_g", "ln1_b", "x1_pow", "x1")
                row_norm(TILES - 1, "ln1_g", "ln1_b", "x1_pow", "x1")

                T = TILES

                def r(a, *dims):
                    n = 1
                    for d in dims:
                        n *= d
                    names = "abc"[:len(dims)]
                    ap = R[:, a:a + n]
                    if len(dims) == 2:
                        ap = ap.rearrange("p (a b) -> p a b", a=dims[0])
                    if len(dims) == 3:
                        ap = ap.rearrange("p (a b c) -> p a b c", a=dims[0], b=dims[1])
                    return ap

                memb = r(0, T, NE)
                lg = r(160, T, 36)
                ex = r(400, T, NG)
                exs = R[:, 400:420]
                ex2 = R[:, 440:445]
                gmax, gsum, smax, m1, m2, s1, s2, den = (R[:, 450 + 5 * k:455 + 5 * k] for k in range(8))
                ohg = r(500, T, NG)
                sc4 = r(520, T, NG)
                esel = r(540, T, EPG)
                oh1 = r(580, T, EPG)
                oh2 = r(620, T, EPG)
                sc8 = r(660, T, EPG)
                e1 = r(700, T, NG, EPG)
                e2 = r(860, T, NG, EPG)
                pos = r(1020, T, NE)
                lap = r(1180, T, NE)
                item = r(1340, T, NE)
                tmp = r(1500, T, NE)
                over = R[:, 1660:1692]
                cs = [R[:, 1692:1740], R[:, 1740:1788]]
                w12 = r(1790, 2, T)
                p12 = r(1800, 2, T)
                sl = r(1810, 2, T)
                eid = R[:, 1820:1820 + NI - NE]
                tot = R[:, 1850:1851]
                hv = R[:, 1852:1852 + 24]

                def bc(ap, dims):
                    return ap.to_broadcast(dims)

                E.need("logits", 1)
                E.link(dve.memset(R[:, 160:340], 0.0))
                E.link(dve.tensor_copy(lg[:, 0:4, :], ps[2][:, 0:144].rearrange("p (t n) -> p t n", t=4)))
                E.link(dve.tensor_copy(lg[0:NS, 4, :], ps[2][0:NS, 144:180]))
                bias = rowpar[:, row_at["router_g_b"][0]:row_at["router_g_b"][0] + 36]
                E.link(dve.tensor_tensor(lg, lg, bc(bias.unsqueeze(1), [128, T, 36]), ALU.add))
                g = lg[:, :, 0:NG]
                E.link(dve.tensor_reduce(gmax, g, AX, ALU.max))
                E.done(dve.tensor_tensor(ex, g, bc(gmax.unsqueeze(2), [128, T, NG]), ALU.subtract), "ex_in")

                def first_max(onehot, values, top, table, score, n):
                    E.link(dve.tensor_tensor(score, values, bc(top.unsqueeze(2), [128, T, n]), ALU.is_equal))
                    E.link(dve.tensor_tensor(score, score, bc(table.unsqueeze(1), [128, T, n]), ALU.mult))
                    E.link(dve.tensor_reduce(smax, score, AX, ALU.max))
                    E.link(dve.tensor_tensor(onehot, score, bc(smax.unsqueeze(2), [128, T, n]), ALU.is_equal))

                first_max(ohg, g, gmax, C("first4"), sc4, NG)
                ev = lg[:, :, NG:36].rearrange("p t (g e) -> p t g e", g=NG)
                E.link(dve.tensor_tensor(e1, ev, bc(ohg.unsqueeze(3), [128, T, NG, EPG]), ALU.mult))
                E.link(dve.tensor_reduce(esel, e1.rearrange("p t g e -> p t e g"), AX, ALU.add))
                E.link(dve.tensor_reduce(m1, esel, AX, ALU.max))
                first_max(oh1, esel, m1, C("first8"), sc8, EPG)
                E.link(dve.scalar_tensor_tensor(out=esel, in0=oh1, scalar=NEG, in1=esel, op0=ALU.mult, op1=ALU.add))
                E.link(dve.tensor_reduce(m2, esel, AX, ALU.max))
                E.done(dve.tensor_tensor(ex2, m2, m1, ALU.subtract), "ex2_in")
                first_max(oh2, esel, m2, C("first8"), sc8, EPG)
                E.need("ex_out", 1)
                E.link(dve.tensor_reduce(gsum, ex, AX, ALU.add))
                E.need("ex2_out", 1)
                E.link(dve.tensor_scalar(den, ex2, 1.0, None, ALU.add))
                E.link(dve.tensor_tensor(den, den, gsum, ALU.mult))
                E.link(dve.reciprocal(gates[:, 0, :], den))
                E.link(dve.tensor_tensor(gates[:, 1, :], gates[:, 0, :], ex2, ALU.mult))
                valid = C("valid")
                for e, oh in ((e1, oh1), (e2, oh2)):
                    E.link(dve.tensor_tensor(e, bc(ohg.unsqueeze(3), [128, T, NG, EPG]), bc(oh.unsqueeze(2), [128, T, NG, EPG]),
                                             ALU.mult))
                    e3 = e.rearrange("p t g e -> p t (g e)")
                    E.link(dve.tensor_tensor(e3, e3, bc(valid.unsqueeze(2), [128, T, NE]), ALU.mult))
                e1f, e2f = (e.rearrange("p t g e -> p t (g e)") for e in (e1, e2))
                E.link(dve.tensor_tensor(memb, e1f, e2f, ALU.add))
                earlier = r(EARLIER, T + 1, NE)
                E.link(dve.memset(earlier[:, 0, :], 0.0))
                for t in range(T):
                    ins = dve.tensor_tensor(earlier[:, t + 1, :], earlier[:, t, :], memb[:, t, :], ALU.add)
                    if t < T - 1:
                        E.link(ins)
                E.done(ins, "member")
                E.need("counts", 1)
                E.link(dve.tensor_scalar(over, ps[4][:, 0:NE], float(BLK), None, ALU.is_gt))
                for k in range(2, (MAXCNT + BLK - 1) // BLK):
                    E.link(dve.scalar_tensor_tensor(out=over, in0=ps[4][:, 0:NE], scalar=float(k * BLK), in1=over,
                                                    op0=ALU.is_gt, op1=ALU.add))
                E.link(dve.memset(cs[0], 0.0))
                E.link(dve.memset(cs[1], 0.0))
                E.link(dve.tensor_copy(cs[0][:, 16:48], over))
                for k, d in enumerate((1, 2, 4, 8, 16)):
                    a, b = cs[k % 2], cs[(k + 1) % 2]
                    E.link(dve.tensor_tensor(b[:, 16:48], a[:, 16:48], a[:, 16 - d:48 - d], ALU.add))
                incl = cs[1][:, 16:48]
                E.need("places", 1)
                E.link(dve.tensor_copy(pos.rearrange("p t e -> p (t e)"), ps[3][:, 0:T * NE]))
                E.link(dve.tensor_scalar(lap, pos, float(BLK), None, ALU.is_ge))
                for k in range(2, (MAXCNT + BLK - 1) // BLK):
                    E.link(dve.scalar_tensor_tensor(out=lap, in0=pos, scalar=float(k * BLK), in1=lap, op0=ALU.is_ge, op1=ALU.add))
                E.link(dve.scalar_tensor_tensor(out=pos, in0=lap, scalar=-float(BLK), in1=pos, op0=ALU.mult, op1=ALU.add))
                eio = C("iota")[:, 0:NE]
                E.link(dve.tensor_tensor(over, incl, over, ALU.subtract))
                E.link(dve.tensor_scalar(over, over, float(NE - 1), None, ALU.add))
                E.link(dve.tensor_tensor(over, over, eio, ALU.subtract))
                E.link(dve.tensor_tensor(item, lap, bc(over.unsqueeze(1), [128, T, NE]), ALU.add))
                E.link(dve.tensor_scalar(tmp, lap, 0.5, None, ALU.is_ge))
                E.link(dve.tensor_tensor(item, item, tmp, ALU.mult))
                E.link(dve.tensor_tensor(item, item, bc(eio.unsqueeze(1), [128, T, NE]), ALU.add))
                for k, e in enumerate((e1f, e2f)):
                    E.link(dve.tensor_tensor(tmp, e, item, ALU.mult))
                    E.link(dve.tensor_reduce(w12[:, k, :], tmp, AX, ALU.add))
                    E.link(dve.tensor_tensor(tmp, e, pos, ALU.mult))
                    E.link(dve.tensor_reduce(p12[:, k, :], tmp, AX, ALU.add))
                E.link(dve.scalar_tensor_tensor(out=sl, in0=w12, scalar=float(BLK), in1=p12, op0=ALU.mult, op1=ALU.add))
                E.link(dve.tensor_copy(slots[:], sl))
                place, whose = onehots(R)
                iota = C("iota")
                for k in range(2):
                    pk = place[:, k * T:(k + 1) * T, :]
                    wk = whose[:, k * T:(k + 1) * T, :]
                    E.link(dve.tensor_tensor(pk, bc(iota.unsqueeze(1), [128, T, 128]), bc(p12[:, k, :].unsqueeze(2), [128, T, 128]),
                                             ALU.is_equal))
                    E.link(dve.tensor_tensor(wk, bc(iota[:, 0:NI].unsqueeze(1), [128, T, NI]),
                                             bc(w12[:, k, :].unsqueeze(2), [128, T, NI]), ALU.is_equal))
                    ins = dve.tensor_tensor(wk, wk, bc(C("tok").unsqueeze(2), [128, T, NI]), ALU.mult)
                    if k == 0:
                        E.link(ins)
                E.done(ins, "onehot")
                nov = NI - NE
                big = R[:, 1020:1020 + nov * NE].rearrange("p (o e) -> p o e", o=nov)
                E.link(dve.tensor_tensor(big, bc(incl.unsqueeze(1), [128, nov, NE]), bc(iota[:, 0:nov].unsqueeze(2), [128, nov, NE]),
                                         ALU.is_le))
                E.link(dve.tensor_reduce(eid, big, AX, ALU.add))
                E.link(dve.tensor_scalar(eid, eid, float(NE - 1), None, ALU.min))
                E.link(dve.tensor_copy(items[0:1, 0:NE], iota[0:1, 0:NE]))
                E.link(dve.tensor_copy(items[0:1, NE:NI], eid[0:1, :]))
                E.link(dve.tensor_scalar(hv[:, 0:nov // 2], iota[:, 0:nov // 2], 2.0, None, ALU.mult))
                E.link(dve.tensor_scalar(hv[:, 0:nov // 2], hv[:, 0:nov // 2], incl[:, NE - 1:NE], None, ALU.is_lt))
                E.link(dve.tensor_reduce(tot, hv[:, 0:nov // 2], AX, ALU.add))
                E.link(dve.tensor_copy(trip[0:1, 0:1], cum[0:1, 0:1]))
                E.link(dve.tensor_scalar(tot, tot, float(NE // 2), None, ALU.add))
                E.link(dve.tensor_tensor(cum[0:1, 0:1], cum[0:1, 0:1], tot[0:1, :], ALU.add))
                E.link(dve.tensor_copy(trip[0:1, 1:2], tot[0:1, :]))
                E.need("idx_ps", 1)
                E.done(dve.tensor_copy(sidx[:], ps[5][:, 0:NI]), "routed")
                E.need("routed", 1)

                lo = dve.value_load(trip[0:1, 0:1], min_val=1, max_val=1 + (DEPTH - 1) * NI // 2)
                turns = dve.value_load(trip[0:1, 1:2], min_val=NE // 2, max_val=NI // 2)
                E.need("x1_store", 16 * TILES)
                for t in range(TILES):
                    ins = dve.tensor_scalar(x[0:ROWS[t], t, :], x[0:ROWS[t], t, :], ALPHA, None, ALU.mult)
                E.link(ins)
                with dve.Fori(0, turns) as turn:
                    i = dve.snap(lo + turn)
                    for q in range(2):
                        dve.wait_ge(sem(f"xg_tr1_{q}"), i + 1)
                        dve.tensor_copy(xgT[q][:, 4:8, :], ps[1][:, 0:4 * BLK].rearrange("p (c m) -> p c m", c=4))\
                           .then_inc(sem(f"xgT_dve{q}"), 1)
                    for q in range(2):
                        dve.wait_ge(sem(f"sg{q}"), i + 1)
                        dve.wait_ge(sem(f"w1_used{q}"), i + 1)
                        dve.tensor_tensor(hm[q], ps[3 + 2 * q][0:BLK, :], sg[q], ALU.mult).then_inc(sem(f"hm{q}"), 1)
                    for q in range(2):
                        dve.wait_ge(sem(f"y1_ps{q}"), i + 1)
                        dve.wait_ge(sem(f"y_stored{q}"), i * 16)
                        dve.tensor_copy(yo[q][:, 512:1024], ps[7][0:BLK, :]).then_inc(sem(f"y_dve{q}"), 1)
                for t in range(TILES):
                    n = ROWS[t]
                    dve.wait_ge(sem(f"y_got{t}"), (L + 1) * 32)
                    for k in range(2):
                        E.link(dve.scalar_tensor_tensor(out=x[0:n, t, :], in0=ygot[t][k][0:n, :], scalar=gates[0:n, k, t:t + 1],
                                                        in1=x[0:n, t, :], op0=ALU.mult, op1=ALU.add))
                    half_stats(t, 0)
                    E.link(half_stats(t, 1))
                    E.link(dve.bn_aggr(mv[0:n, t, 0:2], bn[0:n, t, :, :]))
                    E.done(dve.tensor_scalar(mv[0:n, t, 3:4], mv[0:n, t, 1:2], EPS, None, ALU.add), "x2_stat")
                    if t:
                        row_norm(t - 1, "ln2_g", "ln2_b", "x2_pow", "x2")
                row_norm(TILES - 1, "ln2_g", "ln2_b", "x2_pow", "x2")

        @block.gpsimd
        def _(pool):
            E = Eng(pool, "pool")
            pool.memset(h[:, :, 4, :], 0.0).then_inc(sem("pinit"), 1)
            pool.memset(halfc[:], -0.5).then_inc(sem("pinit"), 1)
            pool.memset(pscr, 0.0).then_inc(sem("pinit"), 1)
            pool.wait_ge(sem("pinit"), 3)
            for q in range(2):
                for name in ("w0_used", "w1_used", "xg_tr0_", "xg_tr1_", "xgT_act", "xgT_dve", "sg", "hm", "hm_tr", "hT",
                             "y0_ps", "y1_ps", "y_act", "y_dve", "gidx"):
                    pool.sem_inc(sem(f"{name}{q}"), 1)
                for name in ("w0_", "w1_", "w2_", "y_stored"):
                    pool.sem_inc(sem(f"{name}{q}"), 16)
            for k in range(NI - NE):
                pool.dma_start(yd[(NE + k) * BLK:(NE + k + 1) * BLK, :], pscr[0:BLK, 0:D]).then_inc(sem("yd_clear"), 16)
            pool.wait_ge(sem("yd_clear"), 16 * (NI - NE))
            pool.wait_ge(start_sem, 16 * (1 + TILES))
            for L in range(DEPTH):
                E.L = L
                st_n = [0]

                def inv_root(n):
                    st_n[0] += 1
                    E.need("st_in", st_n[0])
                    var = pstat[:, n:2 * n]
                    E.done(pool.tensor_tensor(var, var, halfc[:, 0:n], ALU.pow), "st_out")

                E.need("par_in", 32)
                E.link(pool.memset(ctxb[:, :, 0:PAD], 0.0))
                smp = ctxb[:, :, SAMP0:CTXW].rearrange("p c (b w) -> p c b w", b=NB)
                st = CP("conv_state").rearrange("p (c b w) -> p c b w", c=2, b=NB)
                for cb in range(2):
                    E.link(pool.tensor_copy(smp[:, cb, :, 0:PAD], st[:, cb]))
                E.link(pool.memset(smp[:, :, :, PAD:PAD + NT], 0.0))
                E.done(pool.memset(QB, 0.0), "ctx_pool")
                E.need("proj_out", (GATE + 1) * TILES)
                E.done(pool.tensor_tensor(h[:, VAL], h[:, VAL], h[:, GATE], ALU.mult), "glu")
                wT = CP("sgu_wT").rearrange("p (g t) -> p g t", g=4)
                wTs = CP("sgu_wT_s").rearrange("p (g t) -> p g t", g=4)
                E.link(pool.tensor_tensor(wT, wT, C("sgu_mask").unsqueeze(1).to_broadcast([128, 4, 128]), ALU.mult))
                E.done(pool.tensor_tensor(wTs[0:NS], wTs[0:NS], C("sgu_mask_s")[0:NS].unsqueeze(1).to_broadcast([NS, 4, NS]),
                                          ALU.mult), "sgu_w")

                def rotate(s, half_dim, cos, sin):
                    rows = h[:, s].rearrange("p t (h c) -> p t h c", h=NH)
                    n = half_dim
                    a, b = rows[:, :, :, 0:n], rows[:, :, :, n:2 * n]
                    m = TILES * NH * n
                    t1 = pscr[:, 0:m].rearrange("p (t h c) -> p t h c", t=TILES, h=NH)
                    t2 = pscr[:, m:2 * m].rearrange("p (t h c) -> p t h c", t=TILES, h=NH)
                    co = C(cos).rearrange("p (t c) -> p t c", t=TILES)
                    si = C(sin).rearrange("p (t c) -> p t c", t=TILES)
                    for t in range(TILES):
                        cb = co[:, t, :].unsqueeze(1).to_broadcast([128, NH, n])
                        sb_ = si[:, t, :].unsqueeze(1).to_broadcast([128, NH, n])
                        pool.tensor_tensor(t1[:, t], a[:, t], sb_, ALU.mult)
                        pool.tensor_tensor(t2[:, t], b[:, t], sb_, ALU.mult)
                        pool.tensor_tensor(a[:, t], a[:, t], cb, ALU.mult)
                        ins = pool.tensor_tensor(b[:, t], b[:, t], cb, ALU.mult)
                    E.link(ins)
                    E.link(pool.tensor_tensor(a, a, t2, ALU.subtract))
                    ins = pool.tensor_tensor(b, b, t1, ALU.add)
                    return ins

                inv_root(4 * TILES)
                E.need("proj_out", (RK + 1) * TILES)
                E.link(rotate(RQ, 32, "rcos", "rsin"))
                E.done(rotate(RK, 32, "kcos", "ksin"), "rot_r")
                inv_root(TILES)
                E.need("proj_out", (SK + 1) * TILES)
                E.need("rot_r", 1)
                E.link(rotate(SQ, 8, "scos", "ssin"))
                E.done(rotate(SK, 8, "scos", "ssin"), "rot_s")
                E.need("qk_tr", 9)
                kd = C("k_decay").rearrange("p (t h) -> p t h", t=TILES)
                for t in range(TILES):
                    kr = h[:, RK, t, :].rearrange("p (h c) -> p h c", h=NH)
                    ins = pool.tensor_tensor(kr, kr, kd[:, t, :].unsqueeze(2).to_broadcast([128, NH, HD]), ALU.mult)
                E.done(ins, "k_dec")
                E.need("k_dec", 1)
                E.need("conv_tr", 5)
                own = C("own")[0:NS, :]
                for hd in range(NH):
                    vv = h[0:NS, RV, 4, hd * HD:(hd + 1) * HD].unsqueeze(1).to_broadcast([NS, NB, HD])
                    ins = pool.tensor_tensor(vexp[:, hd], vv, own.unsqueeze(2).to_broadcast([NS, NB, HD]), ALU.mult)
                E.done(ins, "vexp")
                E.need("vexp", 1)
                E.need("qk_act", 5)
                for hp in range(2):
                    qb = QB[:, hp, :].rearrange("p (c w) -> p c w", c=4)
                    src = xT[:, 4 + hp, SEQ:NTOK].rearrange("p (c b t) -> p c b t", c=4, b=2)
                    for bb in range(2):
                        for hh in range(2):
                            r = slice(64 * hh, 64 * hh + 64)
                            at = 48 * bb + 4 * (2 * hp + hh)
                            ins = pool.tensor_copy(qb[r, :, at:at + NT], src[r, :, bb, :])
                            if (hp, bb, hh) != (1, 1, 1):
                                E.link(ins)
                E.done(ins, "qb_ok")
                E.need("qb_ok", 1)
                ng = TILES * NH
                rn = h[:, RQ].rearrange("p t (g c) -> p (t g) c", c=HD)
                E.need("ret_mean", 1)
                E.link(pool.tensor_tensor(rn, rn, pstat[:, 0:ng].unsqueeze(2).to_broadcast([128, ng, HD]), ALU.subtract))
                E.done(pool.tensor_tensor(pscr[:, 0:ng * HD].rearrange("p (a c) -> p a c", c=HD), rn, rn, ALU.mult), "ret_sq")
                inv_root(4 * TILES)
                E.need("st_out", 3)
                E.link(pool.tensor_tensor(rn, rn, pstat[:, ng:2 * ng].unsqueeze(2).to_broadcast([128, ng, HD]), ALU.mult))
                gain = RP("ret_gn_g").unsqueeze(1).to_broadcast([128, TILES, 256])
                E.link(pool.tensor_tensor(h[:, RQ], h[:, RQ], gain, ALU.mult))
                E.done(pool.tensor_tensor(h[:, RQ], h[:, RQ], h[:, RG], ALU.mult), "ret_y")
                for t in range(TILES):
                    n = ROWS[t]
                    E.need("x1_stat", t + 1)
                    E.done(pool.tensor_tensor(mv[0:n, t, 2:3], mv[0:n, t, 3:4], halfc[0:n, 0:1], ALU.pow), "x1_pow")
                E.need("routed", 1)
                E.need("x1_store", 16 * TILES)
                lo = pool.value_load(trip[0:1, 0:1], min_val=1, max_val=1 + (DEPTH - 1) * NI // 2)
                turns = pool.value_load(trip[0:1, 1:2], min_val=NE // 2, max_val=NI // 2)
                with pool.Fori(0, turns) as turn:
                    i = pool.snap(lo + turn)
                    for q in range(2):
                        col = pool.snap(turn * 2 + q)
                        pool.wait_ge(sem(f"xg_tr1_{q}"), i)
                        pool.sem_inc(sem(f"gidx{q}"), -1)
                        pool.tensor_copy(gidx[q], sidx[:, bass.ds(col, 1)]).then_inc(sem(f"gidx{q}"), 1)
                        pool.wait_ge(sem(f"gidx{q}"), 1)
                        pool.indirect_dma_start(out=xg[q], out_offset=None, in_=x1d,
                                                in_offset=bass.IndirectOffsetOnAxis(ap=gidx[q], axis=0))\
                            .then_inc(sem(f"xg{q}"), 16)
                for q in range(2):
                    pool.wait_ge(sem(f"y_stored{q}"), (lo + turns) * 16)
                E.link(pool.tensor_tensor(halfc[:, 1:2], halfc[:, 0:1], halfc[:, 2:3], ALU.pow))
                E.link(pool.memset(halfc[:, 1:2], -0.5))
                for t in range(TILES):
                    n = ROWS[t]
                    for k in range(2):
                        pool.indirect_dma_start(out=ygot[t][k][0:n, :], out_offset=None, in_=yd,
                                                in_offset=bass.IndirectOffsetOnAxis(ap=slots[0:n, k, t:t + 1], axis=0))\
                            .then_inc(sem(f"y_got{t}"), 16)
                for t in range(TILES):
                    n = ROWS[t]
                    E.need("x2_stat", t + 1)
                    E.done(pool.tensor_tensor(mv[0:n, t, 2:3], mv[0:n, t, 3:4], halfc[0:n, 0:1], ALU.pow), "x2_pow")

    wrong = {name: (made.get(name, 0), n) for name, n in PER.items() if made.get(name, 0) != n * DEPTH}
    assert not wrong, wrong


def layout(a):
    c = np.ascontiguousarray
    w_in, L = a["w_in"], DEPTH
    order = [7, 8, 9, 10, 3, 0, 1, 2, 4, 5, 6]
    blocks = w_in.reshape(L, KT, 128, NCH, CW)[:, :, :, order]
    proj = blocks.transpose(0, 3, 2, 1, 4)
    outp = a["w_out"].reshape(L, KT, 128, NOUT, CW).transpose(0, 3, 2, 1, 4)
    w_proj = c(np.concatenate([proj, outp], 1)).reshape(L * (NCH + NOUT), 128, KT * CW)

    def keys(cache):
        cache = cache.reshape(L, NB, PAST, 256)
        far = cache[:, :, :512].reshape(L, NB, 32, 16, 256)[:, :, :, :4].reshape(L, NB, 128, 256)
        return np.concatenate([cache[:, :, 512:], far], 2)

    k = keys(a["cache_swa_k"]).transpose(0, 1, 3, 2).reshape(L, NB, 2, 128, NKEY).transpose(0, 1, 3, 2, 4)
    v = keys(a["cache_swa_v"]).reshape(L, NB, 5, 128, 256).transpose(0, 1, 3, 2, 4)
    kv = c(np.concatenate([k.reshape(L, NB, 128, 2 * NKEY), v.reshape(L, NB, 128, 2 * NKEY)], 1))
    row = np.concatenate([a[n].reshape(L, -1) for n, _ in ROWPAR], 1)
    rowpar = c(np.broadcast_to(row[:, None], (L, 128, row.shape[1]))).reshape(L * 128, -1)
    sw = a["sgu_w"].transpose(0, 3, 1, 2)

    def rows128(z):
        full = np.zeros((L, 128) + z.shape[2:], np.float32)
        full[:, :z.shape[1]] = z
        return full

    col = dict(
        conv_w=a["conv_w"].reshape(L, TAPS, 2, 128).transpose(0, 3, 2, 1),
        conv_b=a["conv_b"].reshape(L, 2, 128).transpose(0, 2, 1),
        sgu_wT=sw,
        sgu_wT_s=rows128(np.tile(sw[:, :NT, :, :NT], (1, NB, 1, NB))),
        sgu_b=a["sgu_b"].transpose(0, 2, 1),
        sgu_b_s=rows128(np.tile(a["sgu_b"][:, :, :NT].transpose(0, 2, 1), (1, NB, 1))),
        router_w=np.concatenate([a["router_g_w"], a["router_e_w"].transpose(0, 2, 1, 3).reshape(L, D, NE)], 2)
        .reshape(L, KT, 128, NG + NE).transpose(0, 2, 1, 3),
        conv_state=a["state_conv"].reshape(L, NB, PAD, 2, 128).transpose(0, 4, 3, 1, 2),
        ret_state=a["state_ret"].reshape(L, NB, 2, 2, HD, HD).transpose(0, 3, 4, 2, 1, 5),
    )
    colpar = c(np.concatenate([col[n].reshape(L, 128, -1) for n, _ in COLPAR], 2)).reshape(L * 128, -1)
    return dict(
        x_in=c(np.concatenate([a["x_prompt"].reshape(SEQ, D), a["x_sample"].reshape(NS, D)], 0)),
        w_proj=w_proj, kv=kv.reshape(L * 16, 128, 2 * NKEY), rowpar=rowpar, colpar=colpar,
        w1=a["moe_w1"].reshape(L * NE, 128, KT * FF), w3=a["moe_w3"].reshape(L * NE, 128, KT * FF),
        w2=a["moe_w2"].reshape(L * NE, 128, 4 * D),
    )


OUTS = dict(y=(NTOK, D), p_ret=(DEPTH, 128, 128), s_ret=(DEPTH, 128, 2 * NB * HD), p_k=(DEPTH, SEQ, 256),
            p_v=(DEPTH, SEQ, 256), s_k=(DEPTH, NS, 256), s_v=(DEPTH, NS, 256), p_conv=(DEPTH, PAD, 256),
            s_conv=(DEPTH, NS, 256), s_sgu=(DEPTH, NS, 256))


def kernel(**inputs):
    import concourse.bacc as bacc
    from concourse.bass_utils import run_bass_kernel_spmd

    arrays = layout({k: np.asarray(v) for k, v in inputs.items()})
    arrays["const"] = shape_constants()[0]
    nc = bacc.Bacc("TRN2", target_bir_lowering=False, num_devices=1)
    io = {n: nc.dram_tensor("in_" + n, v.shape, F32, kind="ExternalInput").ap() for n, v in arrays.items()}
    io |= {n: nc.dram_tensor("out_" + n, s, F32, kind="ExternalOutput").ap() for n, s in OUTS.items()}
    io["x1d"] = nc.dram_tensor("x1d", (NTOK, D), F32, kind="Internal").ap()
    io["yd"] = nc.dram_tensor("yd", (NI * BLK, D), F32, kind="Internal").ap()
    trunk_program(nc, io, shape_constants()[1])
    r = run_bass_kernel_spmd(nc, [{"in_" + n: v for n, v in arrays.items()}], core_ids=[0]).results[0]
    o = {n: r["out_" + n] for n in OUTS}
    L = DEPTH
    p_ret = o["p_ret"].reshape(L, 2, HD, 2, HD).transpose(0, 3, 1, 2, 4).reshape(L, 1, NH, HD, HD)
    s_ret = o["s_ret"].reshape(L, 2, HD, 2, NB, HD).transpose(0, 4, 3, 1, 2, 5).reshape(L, NB, NH, HD, HD)
    return (o["y"][:SEQ].reshape(1, SEQ, D), o["y"][SEQ:].reshape(NB, NT, D), p_ret,
            o["p_k"].reshape(L, 1, SEQ, NH, HD), o["p_v"].reshape(L, 1, SEQ, NH, HD), o["p_conv"].reshape(L, 1, PAD, 256),
            s_ret, o["s_k"].reshape(L, NB, NT, NH, HD), o["s_v"].reshape(L, NB, NT, NH, HD),
            o["s_conv"].reshape(L, NB, NT, 256), o["s_sgu"].reshape(L, NB, NT, 256))
```
